# Optimizing a Trainium2 kernel written in Bass

```python
import jax, jax.numpy as jnp
from jax import lax
import numpy as np

D_MODEL = 1024
BATCH = 1
SEQ = 256
DEPTH = 2

MEM_LEN = 256
D_FF = 2816
N_EVEN = (DEPTH + 1) // 2
N_ODD = DEPTH // 2

CONV_A_CH = 512
CONV_A_WIDTH = 31
SWA_HEADS = 8
SWA_KV_HEADS = 2
SWA_GROUP = SWA_HEADS // SWA_KV_HEADS
HEAD_DIM = 64
WINDOW = 128
BLOCK = 128
EVEN_IN = 2 * CONV_A_CH + (SWA_HEADS + 2 * SWA_KV_HEADS) * HEAD_DIM
EVEN_MIX = CONV_A_CH + SWA_HEADS * HEAD_DIM
SC_CH = 1024
SC_WIDTH = 3
XA_HEADS = 4
XA_HEAD_DIM = D_MODEL // XA_HEADS

RMS_EPS = 1e-6
LN_EPS = 1e-5

kernel_name = "hybrid_conformer_swa_shortconv_macaron"

def rmsnorm(x, g):
    x32 = x.astype(jnp.float32)
    y = x32 * lax.rsqrt(jnp.mean(x32 * x32, axis=-1, keepdims=True) + RMS_EPS)
    return y.astype(x.dtype) * g

def layernorm(x, g, b):
    x32 = x.astype(jnp.float32)
    mu = jnp.mean(x32, axis=-1, keepdims=True)
    var = jnp.mean(jnp.square(x32 - mu), axis=-1, keepdims=True)
    y = (x32 - mu) * lax.rsqrt(var + LN_EPS)
    return y.astype(x.dtype) * g + b

def swiglu(u, w_gu, w_down):
    gu = u @ w_gu
    return (jax.nn.silu(gu[..., :D_FF]) * gu[..., D_FF:]) @ w_down

def causal_depthwise_conv(x, w):
    k_width, ch = w.shape
    return lax.conv_general_dilated(
        x, w[:, None, :].astype(x.dtype), window_strides=(1,), padding=[(k_width - 1, 0)],
        dimension_numbers=("NWC", "WIO", "NWC"), feature_group_count=ch)

def alibi_slopes(n_heads):
    return 2.0 ** (-8.0 * jnp.arange(1, n_heads + 1, dtype=jnp.float32) / n_heads)

def conformer_conv(a_val, a_gate, conv_w, conv_b, ln_g, ln_b):
    a = a_val * jax.nn.sigmoid(a_gate)
    a = causal_depthwise_conv(a, conv_w) + conv_b
    return jax.nn.silu(layernorm(a, ln_g, ln_b))

def sliding_window_gqa(q, k, v, sinks):
    bsz, seq = q.shape[:2]
    nb = seq // BLOCK
    qb = q.reshape(bsz, nb, BLOCK, SWA_KV_HEADS, SWA_GROUP, HEAD_DIM)
    kb = k.reshape(bsz, nb, BLOCK, SWA_KV_HEADS, HEAD_DIM)
    vb = v.reshape(bsz, nb, BLOCK, SWA_KV_HEADS, HEAD_DIM)
    pad = ((0, 0), (1, 0), (0, 0), (0, 0), (0, 0))
    kk = jnp.concatenate([jnp.pad(kb, pad)[:, :-1], kb], axis=2)
    vv = jnp.concatenate([jnp.pad(vb, pad)[:, :-1], vb], axis=2)
    scores = jnp.einsum("bnqkgd,bnskd->bnkgqs", qb, kk).astype(jnp.float32) * (HEAD_DIM ** -0.5)
    dist = jnp.arange(BLOCK)[:, None] + BLOCK - jnp.arange(2 * BLOCK)[None, :]
    key_pos = jnp.arange(nb)[:, None] * BLOCK - BLOCK + jnp.arange(2 * BLOCK)[None, :]
    valid = ((dist >= 0) & (dist < WINDOW))[None] & (key_pos >= 0)[:, None, :]
    slopes = alibi_slopes(SWA_HEADS).reshape(SWA_KV_HEADS, SWA_GROUP)
    scores = scores - slopes[:, :, None, None] * dist.astype(jnp.float32)
    scores = jnp.where(valid[None, :, None, None], scores, -jnp.inf)
    sink = jnp.broadcast_to(
        sinks.astype(jnp.float32).reshape(SWA_KV_HEADS, SWA_GROUP)[None, None, :, :, None, None],
        scores.shape[:-1] + (1,))
    probs = jax.nn.softmax(jnp.concatenate([scores, sink], axis=-1), axis=-1)[..., :-1]
    out = jnp.einsum("bnkgqs,bnskd->bnqkgd", probs.astype(vv.dtype), vv)
    return out.reshape(bsz, seq, SWA_HEADS * HEAD_DIM)

def even_mixer(u, w_in, conv_w, conv_b, ln_g, ln_b, sinks, w_out):
    bsz, seq, _ = u.shape
    z = u @ w_in
    o0 = CONV_A_CH
    o1 = o0 + CONV_A_CH
    o2 = o1 + SWA_HEADS * HEAD_DIM
    o3 = o2 + SWA_KV_HEADS * HEAD_DIM
    a = conformer_conv(z[..., :o0], z[..., o0:o1], conv_w, conv_b, ln_g, ln_b)
    q = z[..., o1:o2].reshape(bsz, seq, SWA_KV_HEADS, SWA_GROUP, HEAD_DIM)
    k = z[..., o2:o3].reshape(bsz, seq, SWA_KV_HEADS, HEAD_DIM)
    v = z[..., o3:].reshape(bsz, seq, SWA_KV_HEADS, HEAD_DIM)
    o = sliding_window_gqa(q, k, v, sinks)
    return jnp.concatenate([a, o], axis=-1) @ w_out

def odd_mixer(u, w_in, conv_w, w_out):
    z = u @ w_in
    gate_b = z[..., :SC_CH]
    gate_c = z[..., SC_CH:2 * SC_CH]
    val = z[..., 2 * SC_CH:]
    y = gate_b * causal_depthwise_conv(gate_c * val, conv_w)
    return y @ w_out

def memory_cross_attention(u, m, wq, wkv, wo):
    bsz, seq, _ = u.shape
    mlen = m.shape[1]
    q = (u @ wq).reshape(bsz, seq, XA_HEADS, XA_HEAD_DIM)
    kv = m @ wkv
    k = kv[..., :D_MODEL].reshape(bsz, mlen, XA_HEADS, XA_HEAD_DIM)
    v = kv[..., D_MODEL:].reshape(bsz, mlen, XA_HEADS, XA_HEAD_DIM)
    s = jnp.einsum("bqhd,bkhd->bhqk", q, k).astype(jnp.float32) * (XA_HEAD_DIM ** -0.5)
    p = jax.nn.softmax(s, axis=-1).astype(v.dtype)
    o = jnp.einsum("bhqk,bkhd->bqhd", p, v).reshape(bsz, seq, D_MODEL)
    return o @ wo

def _normal(key, shape, fan_in):
    return jax.random.normal(key, shape, jnp.float32) * (fan_in ** -0.5)

def _gain(key, shape):
    return 1.0 + 0.05 * jax.random.normal(key, shape, jnp.float32)

def setup_inputs(seed: int = 0) -> dict:
    key = jax.random.key(seed)
    ks = jax.random.split(key, 32)
    D, F = D_MODEL, D_FF
    return {
        "x": jax.random.normal(ks[0], (BATCH, SEQ, D), jnp.float32),
        "mem": jax.random.normal(ks[1], (BATCH, MEM_LEN, D), jnp.float32),
        "ffn1_norm": _gain(ks[2], (DEPTH, D)),
        "ffn1_w_gu": _normal(ks[3], (DEPTH, D, 2 * F), D),
        "ffn1_w_down": _normal(ks[4], (DEPTH, F, D), F),
        "mix_norm": _gain(ks[5], (DEPTH, D)),
        "even_w_in": _normal(ks[6], (N_EVEN, D, EVEN_IN), D),
        "conv_a_w": _normal(ks[7], (N_EVEN, CONV_A_WIDTH, CONV_A_CH), CONV_A_WIDTH),
        "conv_a_b": 0.02 * jax.random.normal(ks[8], (N_EVEN, CONV_A_CH), jnp.float32),
        "conv_a_ln_g": _gain(ks[9], (N_EVEN, CONV_A_CH)),
        "conv_a_ln_b": 0.02 * jax.random.normal(ks[10], (N_EVEN, CONV_A_CH), jnp.float32),
        "swa_sinks": 0.5 * jax.random.normal(ks[11], (N_EVEN, SWA_HEADS), jnp.float32),
        "even_w_out": _normal(ks[12], (N_EVEN, EVEN_MIX, D), EVEN_MIX),
        "odd_w_in": _normal(ks[13], (N_ODD, D, 3 * SC_CH), D),
        "sc_conv_w": _normal(ks[14], (N_ODD, SC_WIDTH, SC_CH), SC_WIDTH),
        "odd_w_out": _normal(ks[15], (N_ODD, SC_CH, D), SC_CH),
        "xa_norm": _gain(ks[16], (DEPTH, D)),
        "xa_mem_norm": _gain(ks[17], (DEPTH, D)),
        "xa_wq": _normal(ks[18], (DEPTH, D, D), D),
        "xa_wkv": _normal(ks[19], (DEPTH, D, 2 * D), D),
        "xa_wo": _normal(ks[20], (DEPTH, D, D), D),
        "ffn2_norm": _gain(ks[21], (DEPTH, D)),
        "ffn2_w_gu": _normal(ks[22], (DEPTH, D, 2 * F), D),
        "ffn2_w_down": _normal(ks[23], (DEPTH, F, D), F),
        "final_norm": _gain(ks[24], (D,)),
    }

def reference(x, mem, ffn1_norm, ffn1_w_gu, ffn1_w_down, mix_norm, even_w_in, conv_a_w, conv_a_b,
              conv_a_ln_g, conv_a_ln_b, swa_sinks, even_w_out, odd_w_in, sc_conv_w, odd_w_out,
              xa_norm, xa_mem_norm, xa_wq, xa_wkv, xa_wo, ffn2_norm, ffn2_w_gu, ffn2_w_down, final_norm):
    h = x
    for i in range(DEPTH):
        h = h + 0.5 * swiglu(rmsnorm(h, ffn1_norm[i]), ffn1_w_gu[i], ffn1_w_down[i])
        u = rmsnorm(h, mix_norm[i])
        j = i // 2
        if i % 2 == 0:
            h = h + even_mixer(u, even_w_in[j], conv_a_w[j], conv_a_b[j], conv_a_ln_g[j],
                               conv_a_ln_b[j], swa_sinks[j], even_w_out[j])
        else:
            h = h + odd_mixer(u, odd_w_in[j], sc_conv_w[j], odd_w_out[j])
        h = h + memory_cross_attention(rmsnorm(h, xa_norm[i]), rmsnorm(mem, xa_mem_norm[i]),
                                       xa_wq[i], xa_wkv[i], xa_wo[i])
        h = h + 0.5 * swiglu(rmsnorm(h, ffn2_norm[i]), ffn2_w_gu[i], ffn2_w_down[i])
    return rmsnorm(h, final_norm)


_drawn_inputs = setup_inputs


def setup_inputs(seed=0):
    import zlib

    import numpy as np

    out = dict(_drawn_inputs(seed))
    spreads = {}
    factors = {'conv_a_ln_b': 4.949,
     'swa_sinks': 2.834,
     'xa_norm': 7.617,
     'xa_mem_norm': 5.182,
     'ffn2_norm': 2.915}
    for name, (base, spread) in spreads.items():
        noise = np.random.default_rng([zlib.crc32(name.encode()), seed]).standard_normal(out[name].shape)
        drawn = base * np.exp(spread * noise) if base else spread * noise
        out[name] = __import__('jax').numpy.asarray(drawn.astype(out[name].dtype))
    for name, factor in factors.items():
        out[name] = (out[name] * factor).astype(out[name].dtype)
    return out
```

```python
from collections import defaultdict
from contextlib import ExitStack

import concourse.bass as bass
from concourse import mybir

F32 = mybir.dt.float32
F32R = mybir.dt.float32r
I32 = mybir.dt.int32
ALU = mybir.AluOpType
ACT = mybir.ActivationFunctionType
AX = mybir.AxisListType

P = 128
D = 1024
KD = D // P
HALF = 512
TOK = 256
FF = 2816
FG = 256
GROUPS = FF // FG
CH = 512
TAPS = 31
SC_TAPS = 3
QH, KVH, HD = 8, 2, 64
XH, XHD = 4, 256
MEM = 256
RMS_EPS = 1e-6
LN_EPS = 1e-5
FAR = 1e30

RAW = 4
RING = 12
BLK = 1024
LANDED = 32
TURN_STEPS = 2
TURN_FROM, TURNS = 3, 4
TOTAL_BLOCKS = 4 * (GROUPS * 6) + 2 * 16 + (15 + KD) + (3 * KD + KD) + 2 * (KD + KD)

PER_TURN = {
    "blk": 6 * TURN_STEPS, "blk_used": 5 * TURN_STEPS, "mm": 2 * TURN_STEPS, "mm_read_dve": 2 * TURN_STEPS, "silu": 2 * TURN_STEPS,
    "tr": 2 * TURN_STEPS, "tr_hi": 2 * TURN_STEPS, "tr_read_dve": 2 * TURN_STEPS,
}


class Tally:

    def __init__(self):
        self.n = defaultdict(int)
        self.turn = None

    def at(self, name, back=0):
        v = self.n[name] - back
        return v if self.turn is None else v + self.turn * PER_TURN[name]

    def add(self, name, k=1):
        self.n[name] += k

    def leave_loop(self, turns=TURNS):
        self.turn = None
        for name, k in PER_TURN.items():
            self.n[name] += k * (turns - 1)


def trunk(nc, x, mem, ffn1_norm, ffn1_w_gu, ffn1_w_down, mix_norm, even_w_in, conv_a_w, conv_a_b, conv_a_ln_g,
          conv_a_ln_b, swa_sinks, even_w_out, odd_w_in, sc_conv_w, odd_w_out, xa_norm, xa_mem_norm, xa_wq, xa_wkv,
          xa_wo, ffn2_norm, ffn2_w_gu, ffn2_w_down, final_norm, out):
    ctx = ExitStack()
    with ctx:
        def sb(name, shape, dt=F32):
            return ctx.enter_context(nc.sbuf_tensor(name, shape, dt))

        def ps(name, shape):
            return ctx.enter_context(nc.psum_tensor(name, shape, F32))

        def sem(name):
            return ctx.enter_context(nc.semaphore(name))

        w_raw = sb("w_raw", [P, RAW, BLK])
        w_hi = sb("w_hi", [P, RING, BLK], F32R)
        w_lo = sb("w_lo", [P, RING, BLK], F32R)
        h = sb("h", [P, 2, D])
        act_hi = sb("act_hi", [P, KD, TOK], F32R)
        act_lo = sb("act_lo", [P, KD, TOK], F32R)
        mem_hi = sb("mem_hi", [P, KD, MEM], F32R)
        mem_lo = sb("mem_lo", [P, KD, MEM], F32R)
        hid = sb("hid", [P, 2, FG])
        hidT_hi = sb("hidT_hi", [P, 2, FG // P, P], F32R)
        hidT_lo = sb("hidT_lo", [P, 2, FG // P, P], F32R)
        xn = sb("xn", [P, 2, D])
        gain = sb("gain", [P, D])
        keyT = sb("keyT", [P, KD, MEM])
        val = sb("val", [P, MEM // P, D])
        prmT = sb("prmT", [P, CH // P, 40])
        ident = sb("ident", [P, P])
        ones = sb("ones", [P, P])
        dist = sb("dist", [P, 2 * P])
        half_neg = sb("half_neg", [P, 1])
        ssq = sb("ssq", [P, 2, 2])
        ms = sb("ms", [P, 2])
        rstd = sb("rstd", [P, 2])
        sink = sb("sink", [P, QH])
        top = sb("top", [P, 2, QH])
        neg = sb("neg", [P, 2, QH])
        den = sb("den", [P, 2, QH])
        esink = sb("esink", [P, 2, QH])
        rinv = sb("rinv", [P, 2, QH])
        scratch = sb("scratch", [P, 8056])

        def view(at, *dims):
            n = 1
            for k in dims:
                n *= k
            v = scratch[:, at:at + n]
            if len(dims) == 2:
                v = v.rearrange("p (a b) -> p a b", b=dims[1])
            if len(dims) == 3:
                v = v.rearrange("p (a b c) -> p a b c", b=dims[1], c=dims[2])
            return v

        mem_rows = view(0, 2, D)
        mem_gain = view(2048, D)
        prm = view(3072, CH)
        dist_int = view(3584, 2 * P)
        aT = view(0, CH // P, TAPS - 1 + TOK)
        conv = view(1144, CH // P, TOK)
        swa_qT = view(2168, QH // 2, TOK)
        swa_kT = view(3192, KVH, TOK)
        swa_v = view(3704, 2, KVH * HD)
        swa_p = view(3960, 8 * 2 * P)
        swa_pT = view(6008, 8 * 2 * P)
        sig = view(6008, TOK)
        centred = view(3960, CH // P, TOK)
        squares = view(6008, CH // P, TOK)
        ln_out = view(1144, CH // P, TOK)
        var = view(3960 + 1024, TOK)
        rs = view(3960 + 1024 + 256, TOK)
        pT = view(0, KD, SC_TAPS - 1 + TOK)
        gate_c = view(2064, TOK)
        sc_acc = view(2320, TOK)
        sc_y = view(2832, KD, TOK)
        xa_qT = view(0, KD, TOK)
        xa_p = view(2048, 2, XH, MEM)
        xa_pT = view(4096, 2, XH * 2 * P)

        mm_bank = [ps(f"mm_bank{i}", [P, HALF]) for i in range(2)]
        tr_bank = [ps(f"tr_bank{i}", [P, HALF]) for i in range(2)]
        acc = [ps(f"acc{t}", [P, D]) for t in range(2)]

        raw_landed = [sem(f"raw_landed{i}") for i in range(RAW)]
        blk_hi = sem("blk_hi")
        blk_ready = sem("blk_ready")
        blk_used = sem("blk_used")
        mm_done = sem("mm_done")
        mm_read_dve = sem("mm_read_dve")
        mm_read_act = sem("mm_read_act")
        silu_done = sem("silu_done")
        tr_done = sem("tr_done")
        tr_hi = sem("tr_hi")
        tr_read_dve = sem("tr_read_dve")
        tr_read_act = sem("tr_read_act")
        acc_done = sem("acc_done")
        h_ready = sem("h_ready")
        x_landed = [sem(f"x_landed{t}") for t in range(2)]
        mem_landed = sem("mem_landed")
        gain_landed = sem("gain_landed")
        prm_landed = sem("prm_landed")
        ssq_ready = sem("ssq_ready")
        ms_ready = sem("ms_ready")
        rstd_ready = sem("rstd_ready")
        xn_ready = sem("xn_ready")
        const_ready = sem("const_ready")
        const_step = sem("const_step")
        prm_zero = sem("prm_zero")
        dist_ready = sem("dist_ready")
        prm_ready = sem("prm_ready")
        pad_zero = sem("pad_zero")
        step = sem("step")
        conv_step = sem("conv_step")
        top_ready = sem("top_ready")
        exp_done = sem("exp_done")
        ln_dve = sem("ln_dve")
        ln_act = sem("ln_act")
        ln_pool = sem("ln_pool")
        y_hi = sem("y_hi")
        y_ready = sem("y_ready")
        stored = sem("stored")

        block = ctx.enter_context(nc.Block())

        @block.sync
        def _(sp):
            c = Tally()

            def load(*parts):
                n = c.n["blk"]
                slot = n % RAW
                if n >= RAW:
                    sp.wait_ge(blk_ready, c.at("blk", RAW - 1))
                for i, src in enumerate(parts):
                    inner = src.shape[2] if len(src.shape) == 3 else BLK
                    dst = w_raw[:, slot, :].rearrange("p (a b) -> p a b", b=inner * len(parts))
                    dst = dst[:, :, i * inner:(i + 1) * inner]
                    if len(src.shape) == 2:
                        src = src.unsqueeze(1)
                    sp.dma_start(dst, src).then_inc(raw_landed[slot], LANDED // len(parts))
                c.add("blk")

            def gate_up(w, g):
                v = w.rearrange("(k p) (u f) -> p k u f", p=P, u=2)
                for kk in range(KD // 2):
                    load(*(v[:, 2 * kk:2 * kk + 2, u, bass.ds(g * FG, FG)] for u in range(2)))

            def rows(w, first, n):
                for k in range(n):
                    load(w[bass.ds((first + k) * P, P), :])

            def columns(w, first):
                load(w.rearrange("(k p) n -> p k n", p=P)[:, :, first:first + P])

            def values(w, g):
                v = w.rearrange("(k p) n -> p k n", p=P)
                for kk in range(KD // 2):
                    load(v[:, 2 * kk:2 * kk + 2, D + g * HALF:D + (g + 1) * HALF])

            def load_gain(row):
                if c.n["norms"]:
                    sp.wait_ge(xn_ready, c.n["xn"])
                sp.dma_start(gain[:, :], row.partition_broadcast(P)).then_inc(gain_landed, 16)
                c.add("norms")

            def swiglu(w_gu, w_down, next_gain):
                gate_up(w_gu, 0)
                for g in range(1, TURN_FROM):
                    gate_up(w_gu, g)
                    rows(w_down, (g - 1) * 2, 2)
                with sp.Fori(0, TURNS) as turn:
                    c.turn = turn
                    for u in range(TURN_STEPS):
                        g = turn * TURN_STEPS + (TURN_FROM + u)
                        gate_up(w_gu, g)
                        rows(w_down, g * 2 - 2, 2)
                    c.leave_loop()
                load_gain(next_gain)
                rows(w_down, 2 * (GROUPS - 1), 2)

            for t in range(2):
                sp.dma_start(h[:, t, :], x[0, t * P:(t + 1) * P, :]).then_inc(x_landed[t], 16)
                if t == 0:
                    load_gain(ffn1_norm[0, :])
            for layer in range(2):
                c.add("xn", 8)
                swiglu(ffn1_w_gu[layer], ffn1_w_down[layer], mix_norm[layer, :])
                wkv = xa_wkv[layer]
                for n in range(4):
                    columns(wkv, n * P)
                c.add("xn", 4)
                if layer == 0:
                    w = even_w_in[0]
                    for n in range(CH // P):
                        columns(w, CH + n * P)
                        columns(w, n * P)
                    for n in range(QH * HD // P):
                        columns(w, 2 * CH + n * P)
                    at = 2 * CH + QH * HD
                    for kv in range(KVH):
                        head = w.rearrange("(k p) n -> p k n", p=P)[:, :, at + kv * HD:at + (kv + 1) * HD]
                        load(head, head)
                    columns(w, at + KVH * HD)
                    for n in range(4, KD):
                        columns(wkv, n * P)
                    load_gain(xa_norm[layer, :])
                    values(wkv, 0)
                    rows(even_w_out[0], 0, KD)
                else:
                    w = odd_w_in[0]
                    for n in range(KD):
                        columns(w, D + n * P)
                        columns(w, 2 * D + n * P)
                        columns(w, n * P)
                    load_gain(xa_norm[layer, :])
                    for n in range(4, KD):
                        columns(wkv, n * P)
                    values(wkv, 0)
                    rows(odd_w_out[0], 0, KD)
                values(wkv, 1)
                c.add("xn", 4)
                for n in range(KD):
                    columns(xa_wq[layer], n * P)
                load_gain(ffn2_norm[layer, :])
                c.add("xn", 4)
                rows(xa_wo[layer], 0, KD)
                swiglu(ffn2_w_gu[layer], ffn2_w_down[layer], ffn1_norm[1, :] if layer == 0 else final_norm[:])
            for t in range(2):
                for half in range(2):
                    c.add("xn")
                    sp.wait_ge(xn_ready, c.n["xn"])
                    cols = slice(half * HALF, (half + 1) * HALF)
                    sp.dma_start(out[0, t * P:(t + 1) * P, cols], xn[:, t, cols]).then_inc(stored, 16)
            sp.wait_ge(stored, 64)

        @block.gpsimd
        def _(pool):
            c = Tally()

            def made(ins):
                ins.then_inc(const_step, 1)
                c.add("const")
                pool.wait_ge(const_step, c.n["const"])

            made(nc.gpsimd.memset(half_neg[:, :], -0.5))
            made(nc.gpsimd.memset(ident[:, :], 0.0))
            nc.gpsimd.affine_select(out=ident[:, :], in_=ident[:, :], compare_op=ALU.not_equal, fill=1.0, base=0,
                                    pattern=[[-1, P]], channel_multiplier=1).then_inc(const_ready, 1)
            nc.gpsimd.memset(ones[:, :], 1.0 / CH).then_inc(const_ready, 1)
            nc.gpsimd.iota(dist_int.bitcast(I32), pattern=[[-1, 2 * P]], base=P,
                           channel_multiplier=1).then_inc(const_ready, 1)

            def power(k):
                for _ in range(k):
                    t = c.n["norm"] % 2
                    c.add("norm")
                    pool.wait_ge(ms_ready, c.n["norm"])
                    nc.gpsimd.tensor_tensor(rstd[:, t:t + 1], ms[:, t:t + 1], half_neg[:, :],
                                            ALU.pow).then_inc(rstd_ready, 1)

            power(1)
            pool.wait_ge(dist_ready, 1)
            made(nc.gpsimd.affine_select(out=dist[:, :], in_=dist[:, :], compare_op=ALU.is_ge, fill=FAR, base=P,
                                         pattern=[[-1, 2 * P]], channel_multiplier=1))
            nc.gpsimd.affine_select(out=dist[:, :], in_=dist[:, :], compare_op=ALU.is_ge, fill=FAR, base=-1,
                                    pattern=[[1, 2 * P]], channel_multiplier=-1).then_inc(const_ready, 1)
            power(1)
            power(2)
            power(2)
            pool.wait_ge(ln_dve, 1)
            nc.gpsimd.tensor_tensor(rs, var, half_neg[:, :].broadcast_to([P, TOK]), ALU.pow).then_inc(ln_pool, 1)
            power(2 * 8)

        @block.scalar
        def _(act):
            c = Tally()
            xn_read = [0, 0]

            def split(k, behind=None):
                for _ in range(k):
                    n = c.n["blk"]
                    if n >= TOTAL_BLOCKS:
                        return
                    if behind == "used":
                        c.add("blk_used")
                        act.wait_ge(blk_used, c.at("blk_used"))
                    if behind == "mm":
                        act.wait_ge(mm_done, c.at("mm"))
                    if behind == "acc":
                        act.wait_ge(acc_done, c.n["acc"])
                    landed = LANDED * (n // RAW + 1)
                    if c.turn is not None:
                        landed = landed + c.turn * (LANDED * PER_TURN["blk"] // RAW)
                    act.wait_ge(raw_landed[n % RAW], landed)
                    c.add("blk")
                    nc.scalar.activation(w_hi[:, n % RING, :], w_raw[:, n % RAW, :], ACT.Copy).then_inc(blk_hi, 1)

            def next_mm():
                bank = mm_bank[c.n["mm"] % 2]
                c.add("mm")
                act.wait_ge(mm_done, c.at("mm"))
                return bank

            def next_tr():
                bank = tr_bank[c.n["tr"] % 2]
                c.add("tr")
                act.wait_ge(tr_done, c.at("tr"))
                return bank

            def skip_mm(k=1):
                c.add("mm", k)
                c.add("mm_read_dve", k)

            def silu(t):
                bank = next_mm()
                c.add("mm_read_dve")
                nc.scalar.activation(hid[:, t, :], bank[:, 0:FG], ACT.Silu).then_inc(silu_done, 1)

            def hi_hid(t):
                bank = next_tr()
                c.add("tr_hi")
                nc.scalar.activation(hidT_hi[:, t, :, :], bank[:, 0:FG].rearrange("p (a b) -> p a b", b=P),
                                     ACT.Copy).then_inc(tr_hi, 1)

            def hi_rows(t, dst, chunks=(0, 4)):
                for k in chunks:
                    bank = next_tr()
                    xn_read[t] = c.n["tr"]
                    c.add("tr_hi")
                    nc.scalar.activation(dst[:, k:k + 4, t * P:(t + 1) * P],
                                         bank[:, :].rearrange("p (a b) -> p a b", b=P), ACT.Copy).then_inc(tr_hi, 1)

            def squares_of(t, src, residual):
                if xn_read[t]:
                    act.wait_ge(tr_done, xn_read[t])
                for half in range(2):
                    cols = slice(half * HALF, (half + 1) * HALF)
                    if residual:
                        c.add("h")
                        act.wait_ge(h_ready, c.n["h"])
                    nc.scalar.activation(xn[:, t, cols], src[:, t, cols], ACT.Square, scale=1.0 / D ** 0.5,
                                         accum_out=ssq[:, t, half:half + 1]).then_inc(ssq_ready, 1)

            def copy_mm(dst, cols=HALF):
                bank = next_mm()
                nc.scalar.activation(dst, bank[:, 0:cols], ACT.Copy).then_inc(mm_read_act, 1)

            def copy_tr(dst):
                bank = next_tr()
                nc.scalar.activation(dst, bank[:, :], ACT.Copy).then_inc(tr_read_act, 1)

            def swiglu(with_mem, start, last):
                if start:
                    act.wait_ge(x_landed[1], 16)
                squares_of(1, h, not start)
                if start:
                    split(4)
                silu(0)
                if with_mem:
                    c.add("mem_landed", 48)
                    act.wait_ge(mem_landed, c.n["mem_landed"])
                    squares_of(0, mem_rows, False)
                if start:
                    split(2)
                hi_hid(0)
                silu(0)
                hi_rows(1, act_hi)
                if with_mem:
                    squares_of(1, mem_rows, False)
                    hi_rows(0, mem_hi)
                if start:
                    split(2)
                split(3, "used")
                silu(1)
                split(1, "mm")
                if with_mem:
                    hi_rows(1, mem_hi)
                if start:
                    c.add("tr")
                hi_hid(0)

                def one_step():
                    silu(0)
                    hi_hid(1)
                    split(3, "used")
                    silu(1)
                    split(1, "mm")
                    hi_hid(0)
                    split(2, "used")

                one_step()
                turns = TURNS - 1 if last else TURNS
                with act.Fori(0, turns) as turn:
                    c.turn = turn
                    for _ in range(TURN_STEPS):
                        one_step()
                    c.leave_loop(turns)
                if last:
                    for _ in range(TURN_STEPS):
                        one_step()
                hi_hid(1)
                c.add("acc")
                squares_of(0, h, True)
                split(3, "used")
                silu(1)
                split(1, "mm")
                split(2, "used")
                hi_hid(1)
                if not last:
                    hi_rows(0, act_hi)
                split(1, "used")
                c.add("acc")
                split(1, "acc")

            def out_rows():
                c.add("acc")
                squares_of(0, h, True)
                split(6, "used")
                hi_rows(0, act_hi)
                split(1, "used")
                c.add("acc")
                split(1, "acc")

            def key_copies(k0, k1):
                for k in range(k0, k1):
                    copy_mm(keyT[:, k, :], MEM)
                    split(1, "mm")

            def value_copies(g):
                for m in range(2):
                    copy_mm(val[:, m, g * HALF:(g + 1) * HALF])
                split(4, "mm")

            def mixer_head():
                squares_of(1, h, True)
                key_copies(0, 3)
                hi_rows(1, act_hi)
                key_copies(3, 4)

            def even_mixer():
                mixer_head()
                for n in range(CH // P):
                    bank = next_mm()
                    if n:
                        act.wait_ge(mm_read_dve, c.n["mm_read_dve"])
                    nc.scalar.activation(sig, bank[:, 0:TOK], ACT.Sigmoid).then_inc(mm_read_act, 1)
                    split(1, "mm")
                    skip_mm()
                    split(1, "mm")
                for n in range(QH // 2):
                    copy_mm(swa_qT[:, n, :], TOK)
                    split(1, "mm")
                for n in range(KVH):
                    copy_mm(swa_kT[:, n, :], TOK)
                    split(1, "mm")
                for t in range(2):
                    copy_mm(swa_v[:, t, :], KVH * HD)
                split(1, "mm")

                def exps(t, width):
                    c.add("top")
                    act.wait_ge(top_ready, c.n["top"])
                    for hd in range(QH):
                        e = swa_p[:, hd * width:(hd + 1) * width]
                        nc.scalar.activation(e, e, ACT.Exp, bias=neg[:, t, hd:hd + 1], scale=HD ** -0.5,
                                             accum_out=den[:, t, hd:hd + 1]).then_inc(exp_done, 1)
                    nc.scalar.activation(esink[:, t, :], top[:, t, :], ACT.Exp).then_inc(exp_done, 1)
                    c.add("exp", QH + 1)

                skip_mm(2)
                key_copies(4, 6)
                exps(0, P)
                for n in range(2):
                    copy_tr(swa_pT[:, n * HALF:(n + 1) * HALF])
                skip_mm()
                key_copies(6, 7)
                skip_mm(4)
                key_copies(7, 8)
                hi_rows(0, act_hi, (4,))
                exps(1, 2 * P)
                for n in range(4):
                    copy_tr(swa_pT[:, n * HALF:(n + 1) * HALF])
                skip_mm()
                hi_rows(1, act_hi, (4,))
                skip_mm()
                copy_mm(val[:, 0, 0:HALF])
                act.wait_ge(mm_read_dve, c.n["mm_read_dve"])
                nc.scalar.activation(squares, centred, ACT.Square).then_inc(ln_act, 1)
                c.add("mm")
                copy_mm(val[:, 1, 0:HALF])
                split(4, "mm")
                act.wait_ge(ln_dve, 2)
                for n in range(CH // P):
                    nc.scalar.activation(ln_out[:, n, :], centred[:, n, :], ACT.Silu, bias=prmT[:, n, 33:34],
                                         scale=prmT[:, n, 32:33]).then_inc(ln_act, 1)
                act.wait_ge(ln_act, 1 + CH // P)
                nc.scalar.activation(act_hi[:, 0:4, :], ln_out, ACT.Copy).then_inc(y_hi, 1)
                out_rows()

            def odd_mixer():
                mixer_head()
                y_at = []
                for n in range(KD):
                    bank = next_mm()
                    if n:
                        act.wait_ge(mm_read_dve, c.n["mm_read_dve"] - 1)
                    nc.scalar.activation(gate_c, bank[:, 0:TOK], ACT.Copy).then_inc(mm_read_act, 1)
                    split(1, "mm")
                    for _ in range(2):
                        skip_mm()
                        split(1, "mm")
                    y_at.append(c.n["mm_read_dve"])
                key_copies(4, 8)
                for n in range(2):
                    act.wait_ge(mm_read_dve, y_at[4 * n + 3])
                    nc.scalar.activation(act_hi[:, 4 * n:4 * n + 4, :], sc_y[:, 4 * n:4 * n + 4, :],
                                         ACT.Copy).then_inc(y_hi, 1)
                value_copies(0)
                out_rows()

            def cross_attention():
                squares_of(1, h, True)
                value_copies(1)
                hi_rows(1, act_hi)
                for n in range(KD):
                    copy_mm(xa_qT[:, n, :], TOK)
                    split(1, "mm")
                for t in range(2):
                    for j in range(2):
                        bank = next_mm()
                        c.add("top")
                        act.wait_ge(top_ready, c.n["top"])
                        for i in range(2):
                            hd = 2 * j + i
                            nc.scalar.activation(xa_p[:, t, hd, :], bank[:, i * MEM:(i + 1) * MEM], ACT.Exp,
                                                 bias=neg[:, t, hd:hd + 1], scale=XHD ** -0.5,
                                                 accum_out=den[:, t, hd:hd + 1]).then_inc(exp_done, 1)
                for t in range(2):
                    for j in range(2):
                        copy_tr(xa_pT[:, t, j * HALF:(j + 1) * HALF])
                skip_mm(4)
                hi_rows(0, act_hi)
                hi_rows(1, act_hi)
                out_rows()

            for t in range(2):
                act.dma_start(mem_rows[:, t, :], mem[0, t * P:(t + 1) * P, :]).then_inc(mem_landed, 16)
            act.dma_start(mem_gain, xa_mem_norm[0, :].partition_broadcast(P)).then_inc(mem_landed, 16)
            act.wait_ge(prm_zero, 1)
            act.dma_start(prm[0:TAPS, :], conv_a_w[0]).then_inc(prm_landed, 16)
            act.dma_start(prm[31:32, :], conv_a_b[0:1, :]).then_inc(prm_landed, 16)
            act.dma_start(prm[32:33, :], conv_a_ln_g[0:1, :]).then_inc(prm_landed, 16)
            act.dma_start(prm[33:34, :], conv_a_ln_b[0:1, :]).then_inc(prm_landed, 16)
            for n in range(2):
                act.dma_start(prm[34 + 3 * n:37 + 3 * n, :],
                              sc_conv_w[0][:, n * CH:(n + 1) * CH]).then_inc(prm_landed, 16)
            act.dma_start(sink[:, :], swa_sinks[0, :].partition_broadcast(P)).then_inc(prm_landed, 16)

            act.wait_ge(x_landed[0], 16)
            squares_of(0, h, False)
            split(4)
            hi_rows(0, act_hi)
            swiglu(True, True, False)
            even_mixer()
            cross_attention()
            swiglu(False, False, False)
            for t in range(2):
                act.dma_start(mem_rows[:, t, :], mem[0, t * P:(t + 1) * P, :]).then_inc(mem_landed, 16)
            act.dma_start(mem_gain, xa_mem_norm[1, :].partition_broadcast(P)).then_inc(mem_landed, 16)
            swiglu(True, False, False)
            odd_mixer()
            cross_attention()
            swiglu(False, False, True)
            squares_of(1, h, True)

        @block.vector
        def _(dve):
            c = Tally()

            def split(k):
                for _ in range(k):
                    n = c.n["blk"]
                    if n >= TOTAL_BLOCKS:
                        return
                    c.add("blk")
                    dve.wait_ge(blk_hi, c.at("blk"))
                    nc.vector.tensor_tensor(w_lo[:, n % RING, :], w_raw[:, n % RAW, :],
                                            w_hi[:, n % RING, :].bitcast(F32), ALU.subtract).then_inc(blk_ready, 1)

            def chained(ins):
                ins.then_inc(step, 1)
                c.add("step")
                dve.wait_ge(step, c.n["step"])

            def next_mm():
                bank = mm_bank[c.n["mm"] % 2]
                c.add("mm")
                dve.wait_ge(mm_done, c.at("mm"))
                return bank

            def next_tr():
                bank = tr_bank[c.n["tr"] % 2]
                c.add("tr")
                c.add("tr_hi")
                dve.wait_ge(tr_hi, c.at("tr_hi"))
                return bank

            def skip_mm(k=1):
                c.add("mm", k)
                c.add("mm_read_act", k)

            def gated(t):
                bank = mm_bank[c.n["mm"] % 2]
                c.add("mm")
                c.add("silu")
                dve.wait_ge(silu_done, c.at("silu"))
                c.add("mm_read_dve")
                nc.vector.tensor_tensor(hid[:, t, :], hid[:, t, :], bank[:, FG:2 * FG],
                                        ALU.mult).then_inc(mm_read_dve, 1)

            def lo_hid(t):
                bank = next_tr()
                nc.vector.tensor_tensor(hidT_lo[:, t, :, :], bank[:, 0:FG].rearrange("p (a b) -> p a b", b=P),
                                        hidT_hi[:, t, :, :].bitcast(F32), ALU.subtract).then_inc(tr_read_dve, 1)
                c.add("tr_read_dve")

            def lo_rows(t, dst, hi, chunks=(0, 4)):
                for k in chunks:
                    bank = next_tr()
                    part = slice(t * P, (t + 1) * P)
                    nc.vector.tensor_tensor(dst[:, k:k + 4, part], bank[:, :].rearrange("p (a b) -> p a b", b=P),
                                            hi[:, k:k + 4, part].bitcast(F32),
                                            ALU.subtract).then_inc(tr_read_dve, 1)
                    c.add("tr_read_dve")

            def residual(t, scale):
                c.add("acc")
                dve.wait_ge(acc_done, c.n["acc"])
                for half in range(2):
                    cols = slice(half * HALF, (half + 1) * HALF)
                    nc.vector.scalar_tensor_tensor(out=h[:, t, cols], in0=acc[t][:, cols], scalar=scale,
                                                   in1=h[:, t, cols], op0=ALU.mult,
                                                   op1=ALU.add).then_inc(h_ready, 1)
                c.add("h", 2)

            def mean_square(t, eps=RMS_EPS):
                c.add("ssq", 2)
                dve.wait_ge(ssq_ready, c.n["ssq"])
                nc.vector.tensor_scalar(ms[:, t:t + 1], ssq[:, t, 0:1], ssq[:, t, 1:2], eps, ALU.add,
                                        ALU.add).then_inc(ms_ready, 1)

            def normed(t, src, g, wait_gain=False):
                c.add("norm")
                dve.wait_ge(rstd_ready, c.n["norm"])
                if wait_gain:
                    c.add("gain", 16)
                    dve.wait_ge(gain_landed, c.n["gain"])
                for half in range(2):
                    cols = slice(half * HALF, (half + 1) * HALF)
                    nc.vector.scalar_tensor_tensor(out=xn[:, t, cols], in0=src[:, t, cols], scalar=rstd[:, t:t + 1],
                                                   in1=g[:, cols], op0=ALU.mult, op1=ALU.mult).then_inc(xn_ready, 1)
                c.add("xn", 2)

            def swiglu(scale_before, with_mem, start, last):
                if not start:
                    residual(1, scale_before)
                mean_square(1)
                normed(1, h, gain)
                if start:
                    split(4)
                gated(0)
                if with_mem:
                    mean_square(0)
                    normed(0, mem_rows, mem_gain)
                if start:
                    split(2)
                lo_hid(0)
                gated(0)
                lo_rows(1, act_lo, act_hi)
                if with_mem:
                    mean_square(1)
                    normed(1, mem_rows, mem_gain)
                    lo_rows(0, mem_lo, mem_hi)
                if start:
                    split(2)
                split(3)
                gated(1)
                split(1)
                if with_mem:
                    lo_rows(1, mem_lo, mem_hi)
                if start:
                    bank = tr_bank[c.n["tr"] % 2]
                    c.add("tr")
                    dve.wait_ge(tr_done, c.n["tr"])
                    c.add("tr_read_dve")
                    nc.vector.tensor_copy(prmT[:, :, :], bank[:, :].rearrange("p (a b) -> p a b", b=P)[:, :, 0:40]
                                          ).then_inc(tr_read_dve, 1)
                lo_hid(0)

                def one_step():
                    gated(0)
                    lo_hid(1)
                    split(3)
                    gated(1)
                    split(1)
                    lo_hid(0)
                    split(2)

                one_step()
                turns = TURNS - 1 if last else TURNS
                with dve.Fori(0, turns) as turn:
                    c.turn = turn
                    for _ in range(TURN_STEPS):
                        one_step()
                    c.leave_loop(turns)
                if last:
                    for _ in range(TURN_STEPS):
                        one_step()
                residual(0, 0.5)
                lo_hid(1)
                split(1)
                mean_square(0)
                split(1)
                normed(0, h, gain, True)
                split(1)
                gated(1)
                split(3)
                lo_hid(1)
                if not last:
                    lo_rows(0, act_lo, act_hi)
                split(2)

            def out_rows(scale=1.0):
                residual(0, scale)
                split(1)
                mean_square(0)
                split(1)
                normed(0, h, gain, True)
                split(4)
                lo_rows(0, act_lo, act_hi)
                split(2)

            def mixer_head():
                residual(1, 0.5)
                mean_square(1)
                normed(1, h, gain)
                skip_mm(3)
                split(3)
                lo_rows(1, act_lo, act_hi)
                skip_mm()
                split(1)

            def even_mixer():
                mixer_head()
                nc.vector.memset(aT[:, :, 0:TAPS - 1], 0.0).then_inc(pad_zero, 1)
                dve.wait_ge(pad_zero, 1)
                tokens = []

                def taps():
                    for pair in range(2):
                        for k in range(TAPS):
                            for n in (2 * pair, 2 * pair + 1):
                                if k == 0:
                                    dve.wait_ge(mm_read_dve, tokens[n])
                                    ins = nc.vector.tensor_scalar(conv[:, n, :], aT[:, n, 0:TOK], prmT[:, n, 0:1],
                                                                  prmT[:, n, 31:32], ALU.mult, ALU.add)
                                else:
                                    dve.wait_ge(conv_step, c.n["conv"] - 1)
                                    ins = nc.vector.scalar_tensor_tensor(
                                        out=conv[:, n, :], in0=aT[:, n, k:k + TOK], scalar=prmT[:, n, k:k + 1],
                                        in1=conv[:, n, :], op0=ALU.mult, op1=ALU.add)
                                ins.then_inc(conv_step, 1)
                                c.add("conv")
                                yield

                conv_taps = taps()

                def tap(k):
                    for _ in range(k):
                        next(conv_taps, None)

                for n in range(CH // P):
                    skip_mm()
                    split(1)
                    bank = next_mm()
                    dve.wait_ge(mm_read_act, c.n["mm_read_act"])
                    c.add("mm_read_dve")
                    nc.vector.tensor_tensor(aT[:, n, TAPS - 1:TAPS - 1 + TOK], sig, bank[:, 0:TOK],
                                            ALU.mult).then_inc(mm_read_dve, 1)
                    tokens.append(c.n["mm_read_dve"])
                    split(1)
                    if n >= 2:
                        tap(7)
                for n in range(QH // 2 + KVH + 1):
                    skip_mm()
                    split(1)
                    tap(6)
                skip_mm()

                slopes = [2.0 ** (-8.0 * (hd + 1) / QH) for hd in range(QH)]

                def scores(t, first, count, width):
                    bank = next_mm()
                    c.add("mm_read_dve")
                    away = dist[:, 2 * P - width:2 * P]
                    for i in range(count):
                        hd = first + 2 * i
                        ins = nc.vector.scalar_tensor_tensor(
                            out=swa_p[:, hd * width:(hd + 1) * width], in0=away, scalar=-slopes[hd] * HD ** 0.5,
                            in1=bank[:, i * width:(i + 1) * width], op0=ALU.mult, op1=ALU.add)
                    ins.then_inc(mm_read_dve, 1)
                    dve.wait_ge(mm_read_dve, c.n["mm_read_dve"])
                    heads = slice(first, first + 2 * count - 1, 2)
                    p = swa_p[:, 0:QH * width].rearrange("p (a b) -> p a b", b=width)[:, heads, :]
                    chained(nc.vector.tensor_reduce(top[:, t, heads], p, AX.X, ALU.max))

                def maxima(t):
                    chained(nc.vector.scalar_tensor_tensor(out=neg[:, t, :], in0=top[:, t, :], scalar=HD ** -0.5,
                                                           in1=sink[:, :], op0=ALU.mult, op1=ALU.max))
                    chained(nc.vector.tensor_tensor(top[:, t, :], sink[:, :], neg[:, t, :], ALU.subtract))
                    nc.vector.tensor_scalar(neg[:, t, :], neg[:, t, :], -1.0, None, ALU.mult).then_inc(top_ready, 1)

                def sums(t):
                    c.add("exp", QH + 1)
                    dve.wait_ge(exp_done, c.n["exp"])
                    chained(nc.vector.tensor_tensor(den[:, t, :], den[:, t, :], esink[:, t, :], ALU.add))
                    chained(nc.vector.reciprocal(rinv[:, t, :], den[:, t, :]))

                def heads_out(t):
                    bank = next_mm()
                    c.add("mm_read_dve")
                    nc.vector.tensor_tensor(xn[:, t, 0:HALF].rearrange("p (a b) -> p a b", b=HD),
                                            bank[:, :].rearrange("p (a b) -> p a b", b=HD),
                                            rinv[:, t, :].unsqueeze(2).broadcast_to([P, QH, HD]),
                                            ALU.mult).then_inc(mm_read_dve, 1)

                for odd in range(2):
                    scores(0, odd, 4, P)
                maxima(0)
                for _ in range(2):
                    skip_mm()
                    split(1)
                    tap(6)
                sums(0)
                heads_out(0)
                skip_mm()
                split(1)
                tap(4)
                for j in range(4):
                    scores(1, 4 * (j // 2) + j % 2, 2, 2 * P)
                maxima(1)
                skip_mm()
                split(1)
                c.add("tr", 2)
                lo_rows(0, act_lo, act_hi, (4,))
                tap(10)
                sums(1)
                heads_out(1)
                c.add("tr", 4)
                lo_rows(1, act_lo, act_hi, (4,))
                tap(CH // P * TAPS)
                dve.wait_ge(conv_step, c.n["conv"])
                bank = next_mm()
                c.add("mm_read_dve")
                over_chunks = [P, CH // P, TOK]
                nc.vector.tensor_tensor(centred, conv, bank[:, 0:TOK].unsqueeze(1).broadcast_to(over_chunks),
                                        ALU.subtract).then_inc(mm_read_dve, 1)
                skip_mm()
                bank = next_mm()
                nc.vector.tensor_scalar(var, bank[:, 0:TOK], LN_EPS, None, ALU.add).then_inc(ln_dve, 1)
                dve.wait_ge(ln_pool, 1)
                nc.vector.tensor_tensor(centred, centred, rs.unsqueeze(1).broadcast_to(over_chunks),
                                        ALU.mult).then_inc(ln_dve, 1)
                skip_mm()
                split(4)
                dve.wait_ge(y_hi, 1)
                nc.vector.tensor_tensor(act_lo[:, 0:4, :], ln_out, act_hi[:, 0:4, :].bitcast(F32),
                                        ALU.subtract).then_inc(y_ready, 1)
                out_rows()

            def odd_mixer():
                mixer_head()
                nc.vector.memset(pT[:, :, 0:SC_TAPS - 1], 0.0).then_inc(pad_zero, 1)
                dve.wait_ge(pad_zero, 2)
                for n in range(KD):
                    skip_mm()
                    split(1)
                    bank = next_mm()
                    c.add("mm_read_dve")
                    dve.wait_ge(mm_read_act, c.n["mm_read_act"])
                    nc.vector.tensor_tensor(pT[:, n, SC_TAPS - 1:SC_TAPS - 1 + TOK], gate_c, bank[:, 0:TOK],
                                            ALU.mult).then_inc(mm_read_dve, 1)
                    dve.wait_ge(mm_read_dve, c.n["mm_read_dve"])
                    w = prmT[:, n % 4, 34 + 3 * (n // 4):37 + 3 * (n // 4)]
                    chained(nc.vector.tensor_scalar(sc_acc, pT[:, n, 0:TOK], w[:, 0:1], None, ALU.mult))
                    split(1)
                    for k in range(1, SC_TAPS):
                        chained(nc.vector.scalar_tensor_tensor(out=sc_acc, in0=pT[:, n, k:k + TOK],
                                                               scalar=w[:, k:k + 1], in1=sc_acc, op0=ALU.mult,
                                                               op1=ALU.add))
                    bank = next_mm()
                    c.add("mm_read_dve")
                    nc.vector.tensor_tensor(sc_y[:, n, :], sc_acc, bank[:, 0:TOK], ALU.mult).then_inc(mm_read_dve, 1)
                    split(1)
                dve.wait_ge(mm_read_dve, c.n["mm_read_dve"])
                for n in range(4):
                    skip_mm()
                    split(1)
                for n in range(2):
                    dve.wait_ge(y_hi, 2 + n)
                    nc.vector.tensor_tensor(act_lo[:, 4 * n:4 * n + 4, :], sc_y[:, 4 * n:4 * n + 4, :],
                                            act_hi[:, 4 * n:4 * n + 4, :].bitcast(F32),
                                            ALU.subtract).then_inc(y_ready, 1)
                skip_mm(2)
                split(4)
                out_rows()

            def cross_attention():
                residual(1, 1.0)
                mean_square(1)
                normed(1, h, gain)
                skip_mm(2)
                split(4)
                lo_rows(1, act_lo, act_hi)
                skip_mm(KD)
                split(KD)
                for t in range(2):
                    for j in range(2):
                        bank = next_mm()
                        s = bank[:, :].rearrange("p (a b) -> p a b", b=MEM)
                        part = slice(2 * j, 2 * j + 2)
                        chained(nc.vector.tensor_reduce(top[:, t, part], s, AX.X, ALU.max))
                        nc.vector.tensor_scalar(neg[:, t, part], top[:, t, part], -(XHD ** -0.5), None,
                                                ALU.mult).then_inc(top_ready, 1)
                for t in range(2):
                    c.add("exp", XH)
                    dve.wait_ge(exp_done, c.n["exp"])
                    chained(nc.vector.reciprocal(rinv[:, t, 0:XH], den[:, t, 0:XH]))
                c.add("tr", 4)
                for t in range(2):
                    for j in range(2):
                        bank = next_mm()
                        c.add("mm_read_dve")
                        cols = slice(j * HALF, (j + 1) * HALF)
                        nc.vector.tensor_tensor(
                            xn[:, t, cols].rearrange("p (a b) -> p a b", b=XHD),
                            bank[:, :].rearrange("p (a b) -> p a b", b=XHD),
                            rinv[:, t, 2 * j:2 * j + 2].unsqueeze(2).broadcast_to([P, 2, XHD]),
                            ALU.mult).then_inc(mm_read_dve, 1)
                    if t == 0:
                        lo_rows(0, act_lo, act_hi)
                lo_rows(1, act_lo, act_hi)
                out_rows()

            nc.vector.memset(prm, 0.0).then_inc(prm_zero, 1)
            dve.wait_ge(const_ready, 3)
            nc.vector.tensor_copy(dist[:, :], dist_int.bitcast(I32)).then_inc(dist_ready, 1)
            mean_square(0)
            normed(0, h, gain, True)
            split(4)
            lo_rows(0, act_lo, act_hi)
            swiglu(None, True, True, False)
            even_mixer()
            cross_attention()
            swiglu(1.0, False, False, False)
            swiglu(0.5, True, False, False)
            odd_mixer()
            cross_attention()
            swiglu(1.0, False, False, True)
            residual(1, 0.5)
            mean_square(1)
            normed(1, h, gain)

        @block.tensor
        def _(pe):
            c = Tally()
            mm_free = [None, None]
            tr_free = [None, None]

            def start_mm():
                if c.turn is not None:
                    pe.wait_ge(mm_read_dve, c.at("mm_read_dve", 1))
                elif mm_free[0]:
                    pe.wait_ge(*mm_free[0])
                return mm_bank[c.n["mm"] % 2]

            def end_mm(ins, reader):
                ins.then_inc(mm_done, 1)
                c.add("mm")
                if isinstance(reader, tuple):
                    freed = reader
                elif reader == "dve":
                    c.add("mm_read_dve")
                    freed = (mm_read_dve, c.n["mm_read_dve"])
                else:
                    c.add("mm_read_act")
                    freed = (mm_read_act, c.n["mm_read_act"])
                mm_free[0], mm_free[1] = mm_free[1], freed

            def start_tr():
                if c.turn is not None:
                    pe.wait_ge(tr_read_dve, c.at("tr_read_dve", 1))
                elif tr_free[0]:
                    pe.wait_ge(*tr_free[0])
                return tr_bank[c.n["tr"] % 2]

            def end_tr(ins, reader="dve"):
                ins.then_inc(tr_done, 1)
                c.add("tr")
                name, s = ("tr_read_dve", tr_read_dve) if reader == "dve" else ("tr_read_act", tr_read_act)
                c.add(name)
                tr_free[0], tr_free[1] = tr_free[1], (s, c.n[name])

            def take(n):
                value = n + 1
                if c.turn is not None:
                    value = value + c.turn * PER_TURN["blk"]
                pe.wait_ge(blk_ready, value)

            def products(out_ap, stat, mov, first, last):
                pairs = ((stat[0], mov[0]), (stat[0], mov[1]), (stat[1], mov[0]))
                for i, (a, b) in enumerate(pairs):
                    ins = nc.tensor.matmul(out_ap, a, b, start=first and i == 0, stop=last and i == 2)
                return ins

            def tile_of(pair, k, t):
                return tuple(a[:, k, t * P:(t + 1) * P] for a in pair)

            act_pair, mem_pair = (act_hi, act_lo), (mem_hi, mem_lo)

            def gate_up(t, n, final):
                bank = start_mm()
                for kk in range(4):
                    if not final:
                        take(n + kk)
                    for j in range(2):
                        k = 2 * kk + j
                        cols = slice(j * HALF, (j + 1) * HALF)
                        slot = (n + kk) % RING
                        ins = products(bank[:, :], tile_of(act_pair, k, t), (w_hi[:, slot, cols], w_lo[:, slot, cols]),
                                       k == 0, k == KD - 1)
                    if kk < 3 and final:
                        ins.then_inc(blk_used, 1)
                end_mm(ins, "dve")

            def gu(t, n):
                gate_up(t, n, t == 1)

            def turn_hid(t, job):
                bank = start_tr()
                pe.wait_ge(mm_read_dve, c.at("mm_read_dve", job))
                for i in range(FG // P):
                    ins = nc.tensor.transpose(bank[:, i * P:(i + 1) * P], hid[:, t, i * P:(i + 1) * P], ident[:, :])
                end_tr(ins)

            def down(t, n, back, first=False, last=False):
                pe.wait_ge(tr_read_dve, c.at("tr_read_dve", back))
                for i in range(2):
                    if t == 0:
                        take(n + i)
                    down_chunk(t, n + i, (hidT_hi[:, t, i, :], hidT_lo[:, t, i, :]), first and i == 0,
                               last and i == 1)

            def down_chunk(t, n, stat, first, last):
                slot = n % RING
                for half in range(2):
                    cols = slice(half * HALF, (half + 1) * HALF)
                    ins = products(acc[t][:, cols], stat, (w_hi[:, slot, cols], w_lo[:, slot, cols]), first, last)
                if last:
                    ins.then_inc(acc_done, 1)
                elif t == 1:
                    ins.then_inc(blk_used, 1)

            def acc_free(t):
                if c.n["sums"]:
                    pe.wait_ge(h_ready, 4 * (c.n["sums"] - 1) + 2 * (t + 1))

            def turn_rows(t):
                for k in (0, 4):
                    bank = start_tr()
                    c.add("xn")
                    pe.wait_ge(xn_ready, c.n["xn"])
                    for j in range(4):
                        src = (k + j) * P
                        ins = nc.tensor.transpose(bank[:, j * P:(j + 1) * P], xn[:, t, src:src + P], ident[:, :])
                    end_tr(ins)

            def swiglu(with_mem, start, last):
                n = c.n["blk"]
                sums = c.n["sums"]
                pe.wait_ge(tr_read_dve, c.n["tr_read_dve"])
                gu(0, n)
                gu(0, n + 4)
                turn_hid(0, 1)
                turn_rows(1)
                acc_free(0)
                down(0, n + 8, 2, first=True)
                if with_mem:
                    turn_rows(0)
                pe.wait_ge(tr_read_dve, c.n["tr_read_dve"] - (2 if with_mem else 0))
                gu(1, n)
                if with_mem:
                    turn_rows(1)
                if start:
                    bank = start_tr()
                    pe.wait_ge(prm_landed, 16 * 7)
                    for j in range(4):
                        ins = nc.tensor.transpose(bank[:, j * P:(j + 1) * P], prm[:, j * P:(j + 1) * P], ident[:, :])
                    end_tr(ins)

                turn_hid(0, 1)

                def one_step(m, first=False):
                    gu(0, m)
                    down(0, m + 4, 0)
                    turn_hid(1, 1)
                    gu(1, m - 6)
                    turn_hid(0, 1)
                    if first:
                        acc_free(1)
                    down(1, m - 2, 1, first=first)

                one_step(n + 10, first=True)
                with pe.Fori(0, TURNS) as turn:
                    c.turn = turn
                    for u in range(TURN_STEPS):
                        one_step(n + 16 + 6 * u)
                    c.leave_loop()
                m = n + 4 + 6 * (GROUPS - 1)
                down(0, m, 0, last=True)
                turn_hid(1, 0)
                gu(1, m - 6)
                down(1, m - 2, 0)
                turn_hid(1, 0)
                if not last:
                    turn_rows(0)
                down(1, m, 0 if last else 2, last=True)
                c.n["blk"] = m + 2
                c.add("sums")

            def chunk(pair, reader):
                n = c.n["blk"]
                bank = start_mm()
                take(n)
                slot = n % RING
                for k in range(KD):
                    cols = slice(k * P, (k + 1) * P)
                    ins = products(bank[:, 0:TOK], (w_hi[:, slot, cols], w_lo[:, slot, cols]),
                                   (pair[0][:, k, :], pair[1][:, k, :]), k == 0, k == KD - 1)
                end_mm(ins, reader)
                c.add("blk")

            def values():
                n = c.n["blk"]
                for m in range(2):
                    bank = start_mm()
                    for kk in range(4):
                        take(n + kk)
                        for j in range(2):
                            k = 2 * kk + j
                            cols = slice(j * HALF, (j + 1) * HALF)
                            slot = (n + kk) % RING
                            ins = products(bank[:, :], tile_of(mem_pair, k, m),
                                           (w_hi[:, slot, cols], w_lo[:, slot, cols]), k == 0, k == KD - 1)
                    end_mm(ins, "act")
                    if m == 1:
                        c.add("blk", 4)
                    yield

            def out_rows(hook=None):
                n = c.n["blk"]
                for t in range(2):
                    acc_free(t)
                    if t == 1:
                        pe.wait_ge(tr_read_dve, c.n["tr_read_dve"])
                    for k in range(KD):
                        if t == 0:
                            take(n + k)
                        if t == 0 and k == 2 and hook:
                            hook()
                        if t == 1 and k == 6:
                            turn_rows(0)
                        down_chunk(t, n + k, tile_of(act_pair, k, t), k == 0, k == KD - 1)
                c.add("blk", KD)
                c.add("sums")

            def mixer_head():
                for _ in range(3):
                    chunk(mem_pair, "act")
                turn_rows(1)
                chunk(mem_pair, "act")
                pe.wait_ge(tr_read_dve, c.n["tr_read_dve"])

            def even_mixer():
                mixer_head()
                for _ in range(CH // P):
                    chunk(act_pair, "act")
                    chunk(act_pair, "dve")
                for _ in range(QH // 2 + KVH):
                    chunk(act_pair, "act")
                n = c.n["blk"]
                take(n)
                for t in range(2):
                    bank = start_mm()
                    for k in range(KD):
                        cols = slice(k * P, (k + 1) * P)
                        ins = products(bank[:, 0:P], tile_of(act_pair, k, t),
                                       (w_hi[:, n % RING, cols], w_lo[:, n % RING, cols]), k == 0, k == KD - 1)
                    end_mm(ins, "act")
                c.add("blk")
                in_done = c.n["mm_read_act"]

                def scores(t, first, count):
                    bank = start_mm()
                    pe.wait_ge(mm_read_act, in_done)
                    keys = slice(0, (t + 1) * P)
                    width = (t + 1) * P
                    for i in range(count):
                        hd = first + 2 * i
                        rows = slice(HD * (hd % 2), HD * (hd % 2) + HD)
                        ins = nc.tensor.matmul(bank[:, i * width:(i + 1) * width],
                                               swa_qT[rows, hd // 2, t * P:(t + 1) * P],
                                               swa_kT[rows, hd // (QH // KVH), keys], start=True, stop=True)
                    end_mm(ins, "dve")

                def turn_probs(count, exps):
                    for n in range(count):
                        bank = start_tr()
                        pe.wait_ge(exp_done, exps)
                        for j in range(4):
                            at = n * HALF + j * P
                            ins = nc.tensor.transpose(bank[:, j * P:(j + 1) * P], swa_p[:, at:at + P], ident[:, :])
                        end_tr(ins, "act")

                def heads_out(t):
                    bank = start_mm()
                    pe.wait_ge(tr_read_act, c.n["tr_read_act"])
                    for hd in range(QH):
                        kv = hd // (QH // KVH)
                        for j in range(t + 1):
                            at = (hd * (t + 1) + j) * P
                            ins = nc.tensor.matmul(bank[:, hd * HD:(hd + 1) * HD], swa_pT[:, at:at + P],
                                                   swa_v[:, j, kv * HD:(kv + 1) * HD], start=j == 0, stop=j == t)
                    end_mm(ins, "dve")
                    return c.n["mm_read_dve"]

                def turn_out(t, ready):
                    bank = start_tr()
                    pe.wait_ge(mm_read_dve, ready)
                    for j in range(4):
                        ins = nc.tensor.transpose(bank[:, j * P:(j + 1) * P], xn[:, t, j * P:(j + 1) * P],
                                                  ident[:, :])
                    end_tr(ins)

                for odd in range(2):
                    scores(0, odd, 4)
                chunk(mem_pair, "act")
                chunk(mem_pair, "act")
                turn_probs(2, QH + 1)
                out0 = heads_out(0)
                chunk(mem_pair, "act")
                for j in range(4):
                    scores(1, 4 * (j // 2) + j % 2, 2)
                chunk(mem_pair, "act")
                turn_out(0, out0)
                turn_probs(4, 2 * (QH + 1))
                turn_out(1, heads_out(1))
                bank = start_mm()
                pe.wait_ge(conv_step, CH // P * TAPS)
                for n in range(CH // P):
                    ins = nc.tensor.matmul(bank[:, 0:TOK], ones[:, :], conv[:, n, :], start=n == 0,
                                           stop=n == CH // P - 1)
                end_mm(ins, "dve")
                fill = values()
                next(fill)
                bank = start_mm()
                pe.wait_ge(ln_act, 1)
                for n in range(CH // P):
                    ins = nc.tensor.matmul(bank[:, 0:TOK], ones[:, :], squares[:, n, :], start=n == 0,
                                           stop=n == CH // P - 1)
                end_mm(ins, (ln_dve, 1))
                next(fill)
                pe.wait_ge(y_ready, 1)
                out_rows()

            def odd_mixer():
                mixer_head()
                for _ in range(KD):
                    chunk(act_pair, "act")
                    chunk(act_pair, "dve")
                    chunk(act_pair, "dve")
                for _ in range(4):
                    chunk(mem_pair, "act")
                for _ in values():
                    pass
                pe.wait_ge(y_ready, 3)
                out_rows()

            def cross_attention(n):
                for _ in values():
                    pass
                turn_rows(1)
                pe.wait_ge(tr_read_dve, c.n["tr_read_dve"])
                for _ in range(KD):
                    chunk(act_pair, "act")
                in_done = c.n["mm_read_act"]
                exp_base = 2 * (QH + 1) + 2 * XH * n

                for t in range(2):
                    for j in range(2):
                        bank = start_mm()
                        pe.wait_ge(mm_read_act, in_done)
                        for i in range(2):
                            for k in range(2):
                                q = 2 * (2 * j + i) + k
                                ins = nc.tensor.matmul(bank[:, i * MEM:(i + 1) * MEM], xa_qT[:, q, t * P:(t + 1) * P],
                                                       keyT[:, q, :], start=k == 0, stop=k == 1)
                        end_mm(ins, (exp_done, exp_base + XH * t + 2 * (j + 1)))

                def turn_probs(t, j):
                    bank = start_tr()
                    pe.wait_ge(exp_done, exp_base + XH * t + 2 * (j + 1))
                    for i in range(2):
                        for m in range(2):
                            at = (2 * i + m) * P
                            ins = nc.tensor.transpose(bank[:, at:at + P],
                                                      xa_p[:, t, 2 * j + i, m * P:(m + 1) * P], ident[:, :])
                    end_tr(ins, "act")

                def heads_out(t, j):
                    bank = start_mm()
                    pe.wait_ge(tr_read_act, probs_read[t, j])
                    for i in range(2):
                        hd = 2 * j + i
                        for m in range(2):
                            at = j * HALF + (2 * i + m) * P
                            ins = nc.tensor.matmul(bank[:, i * XHD:(i + 1) * XHD], xa_pT[:, t, at:at + P],
                                                   val[:, m, hd * XHD:(hd + 1) * XHD], start=m == 0, stop=m == 1)
                    end_mm(ins, "dve")

                def turn_out(t):
                    for half in range(2):
                        bank = start_tr()
                        pe.wait_ge(mm_read_dve, out_read[t, half])
                        for j in range(4):
                            at = half * HALF + j * P
                            ins = nc.tensor.transpose(bank[:, j * P:(j + 1) * P], xn[:, t, at:at + P], ident[:, :])
                        end_tr(ins)

                probs_read, out_read = {}, {}
                for t in range(2):
                    for j in range(2):
                        turn_probs(t, j)
                        probs_read[t, j] = c.n["tr_read_act"]
                for t in range(2):
                    for j in range(2):
                        heads_out(t, j)
                        out_read[t, j] = c.n["mm_read_dve"]
                    if t == 0:
                        turn_out(0)
                        operand0 = c.n["tr_read_dve"]
                pe.wait_ge(tr_read_dve, operand0)
                out_rows(lambda: turn_out(1))

            pe.wait_ge(const_ready, 1)
            turn_rows(0)
            swiglu(True, True, False)
            even_mixer()
            cross_attention(0)
            swiglu(False, False, False)
            swiglu(True, False, False)
            odd_mixer()
            cross_attention(1)
            swiglu(False, False, True)


_INS = ["x", "mem", "ffn1_norm", "ffn1_w_gu", "ffn1_w_down", "mix_norm", "even_w_in", "conv_a_w", "conv_a_b",
        "conv_a_ln_g", "conv_a_ln_b", "swa_sinks", "even_w_out", "odd_w_in", "sc_conv_w", "odd_w_out", "xa_norm",
        "xa_mem_norm", "xa_wq", "xa_wkv", "xa_wo", "ffn2_norm", "ffn2_w_gu", "ffn2_w_down", "final_norm"]


def kernel(**inputs):
    import numpy as np
    import concourse.bacc as bacc
    from concourse.bass_utils import run_bass_kernel_spmd

    nc = bacc.Bacc("TRN2", target_bir_lowering=False, num_devices=1, dynamic_dma_scratch_size=1024)
    arrays, args = {}, []
    for name in _INS:
        a = np.ascontiguousarray(inputs[name])
        arrays[f"in_{name}"] = a
        args.append(nc.dram_tensor(f"in_{name}", a.shape, mybir.dt.from_np(a.dtype), kind="ExternalInput").ap())
    out = nc.dram_tensor("out_0", (1, TOK, D), F32, kind="ExternalOutput").ap()
    trunk(nc, *args, out)
    r = run_bass_kernel_spmd(nc, [arrays], core_ids=[0])
    return r.results[0]["out_0"]
```

```python
from collections import defaultdict
from contextlib import ExitStack

import concourse.bass as bass
from concourse import mybir

F32 = mybir.dt.float32
F32R = mybir.dt.float32r
I32 = mybir.dt.int32
ALU = mybir.AluOpType
ACT = mybir.ActivationFunctionType
AX = mybir.AxisListType

P = 128
D = 1024
KD = D // P
HALF = 512
TOK = 256
FF = 2816
FG = 256
GROUPS = FF // FG
CH = 512
TAPS = 31
POOL_TAP = 25
SC_TAPS = 3
QH, KVH, HD = 8, 2, 64
XH, XHD = 4, 256
MEM = 256
RMS_EPS = 1e-6
LN_EPS = 1e-5
FAR = 1e30

RAW = 6
RING = 12
BLK = 1024
LANDED = 32
TURN_STEPS = 2
TURN_FROM, TURNS = 3, 4
QUERY_SPLITS = (1, 1, 1, 2, 1, 2, 1, 2)
TOTAL_BLOCKS = 4 * (GROUPS * 6) + 2 * 16 + (14 + KD) + (3 * KD + KD) + 2 * (KD + KD)

PER_TURN = {
    "blk": 6 * TURN_STEPS, "blk_used": 5 * TURN_STEPS,
    "mm": 2 * TURN_STEPS, "mm_read_dve": 2 * TURN_STEPS, "silu": 2 * TURN_STEPS,
    "tr": 2 * TURN_STEPS, "tr_hi": 2 * TURN_STEPS, "tr_read_dve": 2 * TURN_STEPS,
}


class Tally:

    def __init__(self):
        self.n = defaultdict(int)
        self.turn = None

    def at(self, name, back=0):
        v = self.n[name] - back
        return v if self.turn is None else v + self.turn * PER_TURN[name]

    def add(self, name, k=1):
        self.n[name] += k

    def leave_loop(self, turns=TURNS):
        self.turn = None
        for name, k in PER_TURN.items():
            self.n[name] += k * (turns - 1)


def trunk(nc, x, mem, ffn1_norm, ffn1_w_gu, ffn1_w_down, mix_norm, even_w_in, conv_a_w, conv_a_b, conv_a_ln_g,
          conv_a_ln_b, swa_sinks, even_w_out, odd_w_in, sc_conv_w, odd_w_out, xa_norm, xa_mem_norm, xa_wq, xa_wkv,
          xa_wo, ffn2_norm, ffn2_w_gu, ffn2_w_down, final_norm, out):
    ctx = ExitStack()
    with ctx:
        def sb(name, shape, dt=F32):
            return ctx.enter_context(nc.sbuf_tensor(name, shape, dt))

        def ps(name, shape):
            return ctx.enter_context(nc.psum_tensor(name, shape, F32))

        def sem(name):
            return ctx.enter_context(nc.semaphore(name))

        w_raw = sb("w_raw", [P, RAW, BLK])
        w_hi = sb("w_hi", [P, RING, BLK], F32R)
        w_lo = sb("w_lo", [P, RING, BLK], F32R)
        h = sb("h", [P, 2, D])
        act_hi = sb("act_hi", [P, KD, TOK], F32R)
        act_lo = sb("act_lo", [P, KD, TOK], F32R)
        mem_hi = sb("mem_hi", [P, KD, MEM], F32R)
        mem_lo = sb("mem_lo", [P, KD, MEM], F32R)
        hid = sb("hid", [P, 2, FG])
        hidT_hi = sb("hidT_hi", [P, 2, FG // P, P], F32R)
        hidT_lo = sb("hidT_lo", [P, 2, FG // P, P], F32R)
        xn = sb("xn", [P, 2, D])
        gain = sb("gain", [P, D])
        keyT = sb("keyT", [P, KD, MEM])
        val = sb("val", [P, MEM // P, D])
        prmT = sb("prmT", [P, CH // P, 40])
        ident = sb("ident", [P, P])
        ones = sb("ones", [P, P])
        dist = sb("dist", [P, 2 * P])
        half_neg = sb("half_neg", [P, 1])
        warm = sb("warm", [P, 1])
        ssq = sb("ssq", [P, 2, 2])
        ms = sb("ms", [P, 2])
        rstd = sb("rstd", [P, 2])
        sink = sb("sink", [P, QH])
        top = sb("top", [P, 2, QH])
        neg = sb("neg", [P, 2, QH])
        den = sb("den", [P, 2, QH])
        esink = sb("esink", [P, 2, QH])
        rinv = sb("rinv", [P, 2, QH])
        scratch = sb("scratch", [P, 6776])

        def view(at, *dims):
            n = 1
            for k in dims:
                n *= k
            v = scratch[:, at:at + n]
            if len(dims) == 2:
                v = v.rearrange("p (a b) -> p a b", b=dims[1])
            if len(dims) == 3:
                v = v.rearrange("p (a b c) -> p a b c", b=dims[1], c=dims[2])
            return v

        mem_rows = view(0, 2, D)
        mem_gain = view(2048, D)
        prm = view(3072, CH)
        dist_int = view(3584, 2 * P)
        aT = view(0, CH // P, TAPS - 1 + TOK)
        conv = view(1144, CH // P, TOK)
        swa_qT = view(2168, QH // 2, TOK)
        swa_kT = view(3192, TOK)
        swa_v = xn[:, 0, D - 2 * KVH * HD:D].rearrange("p (a b) -> p a b", b=KVH * HD)
        swa_p = [xn[:, 1, :], view(3704, QH * 2 * P)]
        swa_pT = [view(5752, HALF), view(6264, HALF), val[:, 0, HALF:D], val[:, 1, HALF:D]]
        sig = view(5752, TOK)
        centred = view(3704, CH // P, TOK)
        diag = view(4728, 2, P)
        var = view(4984, 2)
        rs = view(4986, 2)
        squares = view(5752, CH // P, TOK)
        ln_out = view(1144, CH // P, TOK)
        conv_part = xn[:, 0, HALF:HALF + TOK]
        pT = view(0, KD, SC_TAPS - 1 + TOK)
        gate_c = view(2064, TOK)
        sc_acc = view(2320, TOK)
        sc_y = view(2832, KD, TOK)
        xa_qT = view(0, KD, TOK)
        xa_p = view(2048, XH, 2, MEM)
        xa_pT = view(4096, XH, MEM // P, TOK)

        mm_bank = [ps(f"mm_bank{i}", [P, HALF]) for i in range(2)]
        tr_bank = [ps(f"tr_bank{i}", [P, HALF]) for i in range(2)]
        acc = [ps(f"acc{t}", [P, D]) for t in range(2)]

        raw_landed = [sem(f"raw_landed{i}") for i in range(RAW)]
        blk_hi = sem("blk_hi")
        blk_ready = sem("blk_ready")
        blk_used = sem("blk_used")
        mm_done = sem("mm_done")
        mm_read_dve = sem("mm_read_dve")
        mm_read_act = sem("mm_read_act")
        silu_done = sem("silu_done")
        tr_done = sem("tr_done")
        tr_hi = sem("tr_hi")
        tr_read_dve = sem("tr_read_dve")
        tr_read_act = sem("tr_read_act")
        acc_done = sem("acc_done")
        h_ready = sem("h_ready")
        x_landed = [sem(f"x_landed{t}") for t in range(2)]
        mem_landed = sem("mem_landed")
        gain_landed = sem("gain_landed")
        prm_landed = sem("prm_landed")
        ssq_ready = sem("ssq_ready")
        ms_ready = sem("ms_ready")
        rstd_ready = sem("rstd_ready")
        xn_ready = sem("xn_ready")
        const_ready = sem("const_ready")
        const_step = sem("const_step")
        prm_zero = sem("prm_zero")
        dist_ready = sem("dist_ready")
        pad_zero = sem("pad_zero")
        step = sem("step")
        conv_step = sem("conv_step")
        top_ready = sem("top_ready")
        exp_done = sem("exp_done")
        probs_ready = sem("probs_ready")
        out_hi = sem("out_hi")
        tap_product = sem("tap_product")
        pool_conv = sem("pool_conv")
        scaled = sem("scaled")
        ln_dve = sem("ln_dve")
        ln_act = sem("ln_act")
        ln_pool = sem("ln_pool")
        y_hi = sem("y_hi")
        y_ready = sem("y_ready")
        stored = sem("stored")

        block = ctx.enter_context(nc.Block())

        @block.sync
        def _(sp):
            c = Tally()

            def load(*parts):
                n = c.n["blk"]
                slot = n % RAW
                if n >= RAW:
                    sp.wait_ge(blk_ready, c.at("blk", RAW - 1))
                for i, src in enumerate(parts):
                    inner = src.shape[2] if len(src.shape) == 3 else BLK
                    dst = w_raw[:, slot, :].rearrange("p (a b) -> p a b", b=inner * len(parts))
                    dst = dst[:, :, i * inner:(i + 1) * inner]
                    if len(src.shape) == 2:
                        src = src.unsqueeze(1)
                    sp.dma_start(dst, src).then_inc(raw_landed[slot], LANDED // len(parts))
                c.add("blk")

            def gate_up(w, g):
                v = w.rearrange("(k p) (u f) -> p k u f", p=P, u=2)
                for kk in range(KD // 2):
                    load(*(v[:, 2 * kk:2 * kk + 2, u, bass.ds(g * FG, FG)] for u in range(2)))

            def rows(w, first, n):
                for k in range(n):
                    load(w[bass.ds((first + k) * P, P), :])

            def columns(w, first):
                load(w.rearrange("(k p) n -> p k n", p=P)[:, :, first:first + P])

            def values(w, g):
                v = w.rearrange("(k p) n -> p k n", p=P)
                for kk in range(KD // 2):
                    load(v[:, 2 * kk:2 * kk + 2, D + g * HALF:D + (g + 1) * HALF])

            def load_gain(row):
                if c.n["norms"]:
                    sp.wait_ge(xn_ready, c.n["xn"])
                sp.dma_start(gain[:, :], row.partition_broadcast(P)).then_inc(gain_landed, 16)
                c.add("norms")

            def swiglu(w_gu, w_down, next_gain, start=False):
                gate_up(w_gu, 0)
                if start:
                    load_x(1)
                for g in range(1, TURN_FROM):
                    gate_up(w_gu, g)
                    rows(w_down, (g - 1) * 2, 2)
                    if start and g == 1:
                        load_small()
                with sp.Fori(0, TURNS) as turn:
                    c.turn = turn
                    for u in range(TURN_STEPS):
                        g = turn * TURN_STEPS + (TURN_FROM + u)
                        gate_up(w_gu, g)
                        rows(w_down, g * 2 - 2, 2)
                    c.leave_loop()
                load_gain(next_gain)
                rows(w_down, 2 * (GROUPS - 1), 2)

            def load_small():
                sp.wait_ge(prm_zero, 1)
                sp.dma_start(prm[0:TAPS, :], conv_a_w[0]).then_inc(prm_landed, 16)
                sp.dma_start(prm[31:32, :], conv_a_b[0:1, :]).then_inc(prm_landed, 16)
                sp.dma_start(prm[32:33, :], conv_a_ln_g[0:1, :]).then_inc(prm_landed, 16)
                sp.dma_start(prm[33:34, :], conv_a_ln_b[0:1, :]).then_inc(prm_landed, 16)
                for n in range(2):
                    sp.dma_start(prm[34 + 3 * n:37 + 3 * n, :],
                                 sc_conv_w[0][:, n * CH:(n + 1) * CH]).then_inc(prm_landed, 16)
                sp.dma_start(sink[:, :], swa_sinks[0, :].partition_broadcast(P)).then_inc(prm_landed, 16)
                for t in range(2):
                    sp.dma_start(mem_rows[:, t, :], mem[0, t * P:(t + 1) * P, :]).then_inc(mem_landed, 16)
                sp.dma_start(mem_gain, xa_mem_norm[0, :].partition_broadcast(P)).then_inc(mem_landed, 16)

            def load_x(t):
                sp.dma_start(h[:, t, :], x[0, t * P:(t + 1) * P, :]).then_inc(x_landed[t], 16)
            load_x(0)
            load_gain(ffn1_norm[0, :])
            for layer in range(2):
                c.add("xn", 8)
                swiglu(ffn1_w_gu[layer], ffn1_w_down[layer], mix_norm[layer, :], layer == 0)
                wkv = xa_wkv[layer]
                for n in range(4):
                    columns(wkv, n * P)
                c.add("xn", 4)
                if layer == 0:
                    w = even_w_in[0]
                    for n in range(CH // P):
                        columns(w, CH + n * P)
                        columns(w, n * P)
                    by_head = w[:, 2 * CH:2 * CH + QH * HD].rearrange("(k p) (a b) -> p k a b", p=P, b=HD)
                    for n in range(QH // KVH):
                        load(*(by_head[:, :, n + kv * (QH // KVH), :] for kv in range(KVH)))
                    at = 2 * CH + QH * HD
                    columns(w, at)
                    columns(w, at + KVH * HD)
                    for n in range(4, KD):
                        columns(wkv, n * P)
                    load_gain(xa_norm[layer, :])
                    values(wkv, 0)
                    rows(even_w_out[0], 4, 4)
                    rows(even_w_out[0], 0, 4)
                else:
                    w = odd_w_in[0]
                    for n in range(KD):
                        columns(w, D + n * P)
                        columns(w, 2 * D + n * P)
                        columns(w, n * P)
                    load_gain(xa_norm[layer, :])
                    for n in range(4, KD):
                        columns(wkv, n * P)
                    values(wkv, 0)
                    rows(odd_w_out[0], 0, KD)
                values(wkv, 1)
                c.add("xn", 4)
                for n in range(KD):
                    columns(xa_wq[layer], n * P)
                load_gain(ffn2_norm[layer, :])
                c.add("xn", 4)
                rows(xa_wo[layer], 0, KD)
                swiglu(ffn2_w_gu[layer], ffn2_w_down[layer], ffn1_norm[1, :] if layer == 0 else final_norm[:])
            for t in range(2):
                for half in range(2):
                    c.add("xn")
                    sp.wait_ge(xn_ready, c.n["xn"])
                    cols = slice(half * HALF, (half + 1) * HALF)
                    sp.dma_start(out[0, t * P:(t + 1) * P, cols], xn[:, t, cols]).then_inc(stored, 16)
            sp.wait_ge(stored, 64)

        @block.gpsimd
        def _(pool):
            c = Tally()

            def made(ins):
                ins.then_inc(const_step, 1)
                c.add("const")
                pool.wait_ge(const_step, c.n["const"])

            made(nc.gpsimd.memset(half_neg[:, :], -0.5))
            made(nc.gpsimd.memset(ident[:, :], 0.0))
            nc.gpsimd.affine_select(out=ident[:, :], in_=ident[:, :], compare_op=ALU.not_equal, fill=1.0, base=0,
                                    pattern=[[-1, P]], channel_multiplier=1).then_inc(const_ready, 1)
            nc.gpsimd.memset(ones[:, :], 1.0 / CH).then_inc(const_ready, 1)
            nc.gpsimd.iota(dist_int.bitcast(I32), pattern=[[-1, 2 * P]], base=P,
                           channel_multiplier=1).then_inc(const_ready, 1)

            def power(k):
                for _ in range(k):
                    t = c.n["norm"] % 2
                    c.add("norm")
                    pool.wait_ge(ms_ready, c.n["norm"])
                    nc.gpsimd.tensor_tensor(rstd[:, t:t + 1], ms[:, t:t + 1], half_neg[:, :],
                                            ALU.pow).then_inc(rstd_ready, 1)

            power(1)
            pool.wait_ge(dist_ready, 1)
            made(nc.gpsimd.affine_select(out=dist[:, :], in_=dist[:, :], compare_op=ALU.is_ge, fill=FAR, base=P,
                                         pattern=[[-1, 2 * P]], channel_multiplier=1))
            nc.gpsimd.affine_select(out=dist[:, :], in_=dist[:, :], compare_op=ALU.is_ge, fill=FAR, base=-1,
                                    pattern=[[1, 2 * P]], channel_multiplier=-1).then_inc(const_ready, 1)
            power(1)
            power(2)
            power(2)
            def convolved(n, to, k0, k1):
                pool.wait_ge(mm_read_dve, 2 * GROUPS + 1 + n)
                done = c.n["pool_conv"]
                if done:
                    pool.wait_ge(pool_conv, done)

                def tap_of(k):
                    nc.gpsimd.tensor_scalar(hid[:, k % 2, :], aT[:, n, k:k + TOK], prmT[:, n, k:k + 1], None,
                                            ALU.mult).then_inc(tap_product, 1)

                nc.gpsimd.tensor_scalar(to, aT[:, n, k0:k0 + TOK], prmT[:, n, k0:k0 + 1],
                                        prmT[:, n, 31:32] if k0 == 0 else 0.0, ALU.mult, ALU.add).then_inc(pool_conv, 1)
                tap_of(k0 + 1)
                for k in range(k0 + 1, k1):
                    pool.wait_ge(pool_conv, done + k - k0)
                    if k + 1 < k1:
                        tap_of(k + 1)
                    c.add("tap_product")
                    pool.wait_ge(tap_product, c.n["tap_product"])
                    nc.gpsimd.tensor_tensor(to, to, hid[:, k % 2, :], ALU.add).then_inc(pool_conv, 1)
                c.add("pool_conv", k1 - k0)

            convolved(0, conv[:, 0, :], 0, TAPS)
            convolved(3, conv_part, POOL_TAP, TAPS)
            pool.wait_ge(ln_dve, 1)
            nc.gpsimd.tensor_tensor(rs, var, half_neg[:, :].broadcast_to([P, 2]), ALU.pow).then_inc(ln_pool, 1)
            power(2 * 8)

        @block.scalar
        def _(act):
            c = Tally()
            xn_read = [0, 0]

            def split(k, behind=None):
                for _ in range(k):
                    n = c.n["blk"]
                    if n >= TOTAL_BLOCKS:
                        return
                    if behind == "used":
                        c.add("blk_used")
                        act.wait_ge(blk_used, c.at("blk_used"))
                    if behind == "mm":
                        act.wait_ge(mm_done, c.at("mm"))
                    if behind == "acc":
                        act.wait_ge(acc_done, c.n["acc"])
                    landed = LANDED * (n // RAW + 1)
                    if c.turn is not None:
                        landed = landed + c.turn * (LANDED * PER_TURN["blk"] // RAW)
                    act.wait_ge(raw_landed[n % RAW], landed)
                    c.add("blk")
                    nc.scalar.activation(w_hi[:, n % RING, :], w_raw[:, n % RAW, :], ACT.Copy).then_inc(blk_hi, 1)

            def load_table(function):
                act.wait_ge(const_ready, 1)
                nc.scalar.activation(warm[:, :], half_neg[:, :], function)

            def next_mm():
                bank = mm_bank[c.n["mm"] % 2]
                c.add("mm")
                act.wait_ge(mm_done, c.at("mm"))
                return bank

            def next_tr():
                bank = tr_bank[c.n["tr"] % 2]
                c.add("tr")
                act.wait_ge(tr_done, c.at("tr"))
                return bank

            def skip_mm(k=1):
                c.add("mm", k)
                c.add("mm_read_dve", k)

            def silu(t):
                bank = next_mm()
                c.add("mm_read_dve")
                nc.scalar.activation(hid[:, t, :], bank[:, 0:FG], ACT.Silu).then_inc(silu_done, 1)

            def hi_hid(t):
                bank = next_tr()
                c.add("tr_hi")
                nc.scalar.activation(hidT_hi[:, t, :, :], bank[:, 0:FG].rearrange("p (a b) -> p a b", b=P),
                                     ACT.Copy).then_inc(tr_hi, 1)

            def hi_rows(t, dst, chunks=(0, 4)):
                for k in chunks:
                    bank = next_tr()
                    xn_read[t] = c.n["tr"]
                    c.add("tr_hi")
                    nc.scalar.activation(dst[:, k:k + 4, t * P:(t + 1) * P],
                                         bank[:, :].rearrange("p (a b) -> p a b", b=P), ACT.Copy).then_inc(tr_hi, 1)

            def squares_of(t, src, residual):
                if xn_read[t]:
                    act.wait_ge(tr_done, xn_read[t])
                for half in range(2):
                    cols = slice(half * HALF, (half + 1) * HALF)
                    if residual:
                        c.add("h")
                        act.wait_ge(h_ready, c.n["h"])
                    nc.scalar.activation(xn[:, t, cols], src[:, t, cols], ACT.Square, scale=1.0 / D ** 0.5,
                                         accum_out=ssq[:, t, half:half + 1]).then_inc(ssq_ready, 1)

            def copy_mm(dst, cols=HALF):
                bank = next_mm()
                nc.scalar.activation(dst, bank[:, 0:cols], ACT.Copy).then_inc(mm_read_act, 1)

            def copy_tr(dst):
                bank = next_tr()
                nc.scalar.activation(dst, bank[:, :], ACT.Copy).then_inc(tr_read_act, 1)

            def swiglu(with_mem, start, last):
                if start:
                    act.wait_ge(x_landed[1], 16)
                squares_of(1, h, not start)
                if start:
                    split(4)
                silu(0)
                if start:
                    split(2)
                hi_hid(0)
                silu(0)
                hi_rows(1, act_hi)
                if start:
                    split(2)
                split(3, "used")
                silu(1)
                split(1, "mm")
                if start:
                    c.add("tr")
                hi_hid(0)
                if with_mem:
                    c.add("mem_landed", 48)
                    act.wait_ge(mem_landed, c.n["mem_landed"])
                    squares_of(0, mem_rows, False)

                def one_step(with_mem=False):
                    silu(0)
                    if with_mem:
                        squares_of(1, mem_rows, False)
                    hi_hid(1)
                    if with_mem:
                        hi_rows(0, mem_hi)
                    split(3, "used")
                    silu(1)
                    split(1, "mm")
                    hi_hid(0)
                    split(2, "used")
                    if with_mem:
                        hi_rows(1, mem_hi)

                one_step(with_mem)
                turns = TURNS - 1 if last else TURNS
                with act.Fori(0, turns) as turn:
                    c.turn = turn
                    for _ in range(TURN_STEPS):
                        one_step()
                    c.leave_loop(turns)
                if last:
                    for _ in range(TURN_STEPS):
                        one_step()
                hi_hid(1)
                c.add("acc")
                squares_of(0, h, True)
                split(3, "used")
                silu(1)
                split(1, "mm")
                hi_hid(1)
                split(2, "used")
                if not last:
                    hi_rows(0, act_hi)
                split(1, "used")
                c.add("acc")
                split(1, "acc")

            def out_rows(turn_inside=False):
                c.add("acc")
                squares_of(0, h, True)
                split(4, "used")
                if turn_inside:
                    hi_rows(0, act_hi)
                split(3, "used")
                c.add("acc")
                split(1, "acc")

            def key_copies(k0, k1):
                for k in range(k0, k1):
                    copy_mm(keyT[:, k, :], MEM)
                    split(1, "mm")

            def value_copies(g):
                for m in range(2):
                    copy_mm(val[:, m, g * HALF:(g + 1) * HALF])
                split(4, "mm")

            def mixer_head():
                squares_of(1, h, True)
                key_copies(0, 3)
                hi_rows(1, act_hi)
                key_copies(3, 4)

            def even_mixer():
                mixer_head()
                for n in range(CH // P):
                    bank = next_mm()
                    if n:
                        act.wait_ge(mm_read_dve, c.n["mm_read_dve"])
                    nc.scalar.activation(sig, bank[:, 0:TOK], ACT.Sigmoid).then_inc(mm_read_act, 1)
                    split(1, "mm")
                    skip_mm()
                    split(1, "mm")
                for n in range(QH // 2):
                    copy_mm(swa_qT[:, n, :], TOK)
                    split(1, "mm")
                copy_mm(swa_kT, TOK)
                split(1, "mm")
                for t in range(2):
                    copy_mm(swa_v[:, t, :], KVH * HD)
                split(1, "mm")

                def exps(t, width):
                    c.add("top")
                    act.wait_ge(top_ready, c.n["top"])
                    for hd in range(QH):
                        e = swa_p[t][:, hd * width:(hd + 1) * width]
                        nc.scalar.activation(e, e, ACT.Exp, bias=neg[:, t, hd:hd + 1], scale=HD ** -0.5,
                                             accum_out=den[:, t, hd:hd + 1]).then_inc(exp_done, 1)
                    nc.scalar.activation(esink[:, t, :], top[:, t, :], ACT.Exp).then_inc(exp_done, 1)
                    c.add("exp", QH + 1)

                key_copies(4, 5)
                skip_mm(2)
                key_copies(5, 6)
                exps(0, P)
                skip_mm(2)
                key_copies(6, 7)
                for n in range(2):
                    copy_tr(swa_pT[n])
                skip_mm(3)
                exps(1, 2 * P)
                key_copies(7, 8)
                hi_rows(0, act_hi, (4,))
                copy_mm(val[:, 0, 0:HALF])
                for n in range(2):
                    copy_tr(swa_pT[n])
                copy_mm(val[:, 1, 0:HALF])
                for n in range(2, 4):
                    copy_tr(swa_pT[n])
                split(4, "mm")
                skip_mm()
                hi_rows(1, act_hi, (4,))
                skip_mm()
                act.wait_ge(mm_read_dve, c.n["mm_read_dve"])
                nc.scalar.activation(squares, centred, ACT.Square).then_inc(ln_act, 1)
                load_table(ACT.Silu)
                split(1, "used")
                c.add("mm", 2)

                def y_part(n):
                    act.wait_ge(ln_act, 2 + n)
                    nc.scalar.activation(act_hi[:, n, :], ln_out[:, n, :], ACT.Copy).then_inc(y_hi, 1)

                for n in range(CH // P):
                    act.wait_ge(scaled, n + 1)
                    nc.scalar.activation(ln_out[:, n, :], centred[:, n, :], ACT.Silu, bias=prmT[:, n, 33:34],
                                         scale=prmT[:, n, 32:33]).then_inc(ln_act, 1)
                    y_part(n)
                split(3, "used")
                c.add("acc")
                squares_of(0, h, True)
                split(3, "used")
                c.add("acc")
                split(1, "acc")

            def odd_mixer():
                mixer_head()
                y_at = []
                for n in range(KD):
                    bank = next_mm()
                    if n:
                        act.wait_ge(mm_read_dve, c.n["mm_read_dve"] - 1)
                    nc.scalar.activation(gate_c, bank[:, 0:TOK], ACT.Copy).then_inc(mm_read_act, 1)
                    split(1, "mm")
                    for _ in range(2):
                        skip_mm()
                        split(1, "mm")
                    y_at.append(c.n["mm_read_dve"])
                key_copies(4, 8)
                for n in range(2):
                    act.wait_ge(mm_read_dve, y_at[4 * n + 3])
                    nc.scalar.activation(act_hi[:, 4 * n:4 * n + 4, :], sc_y[:, 4 * n:4 * n + 4, :],
                                         ACT.Copy).then_inc(y_hi, 1)
                value_copies(0)
                out_rows()

            def cross_attention():
                squares_of(1, h, True)
                copy_mm(val[:, 0, HALF:D])
                hi_rows(0, act_hi)
                load_table(ACT.Exp)
                hi_rows(1, act_hi)
                copy_mm(val[:, 1, HALF:D])
                split(1, "mm")

                def exps(hd):
                    bank = next_mm()
                    c.add("top")
                    act.wait_ge(top_ready, c.n["top"])
                    for t in range(2):
                        nc.scalar.activation(xa_p[:, hd, t, :], bank[:, t * MEM:(t + 1) * MEM], ACT.Exp,
                                             bias=neg[:, t, hd:hd + 1], scale=XHD ** -0.5,
                                             accum_out=den[:, t, hd:hd + 1]).then_inc(exp_done, 1)

                def hi_out(hd):
                    bank = next_mm()
                    c.add("mm_read_dve")
                    nc.scalar.activation(mem_hi[:, 2 * hd:2 * hd + 2, :],
                                         bank[:, :].rearrange("p (a b) -> p a b", b=TOK), ACT.Copy).then_inc(out_hi, 1)

                def copy_probs(hd):
                    bank = next_tr()
                    nc.scalar.activation(xa_pT[:, hd, :, :], bank[:, :].rearrange("p (a b) -> p a b", b=TOK),
                                         ACT.Copy).then_inc(tr_read_act, 1)

                def queries(n):
                    copy_mm(xa_qT[:, n, :], TOK)
                    split(QUERY_SPLITS[n], "mm")

                queries(0)
                for hd in range(XH):
                    queries(2 * hd + 1)
                    if hd + 1 < XH:
                        queries(2 * hd + 2)
                    if hd >= 2:
                        hi_out(hd - 2)
                    if hd >= 1:
                        copy_probs(hd - 1)
                    exps(hd)
                hi_out(XH - 2)
                copy_probs(XH - 1)
                hi_out(XH - 1)
                out_rows(True)

            act.wait_ge(x_landed[0], 16)
            squares_of(0, h, False)
            split(1)
            hi_rows(0, act_hi)
            split(3)
            swiglu(True, True, False)
            even_mixer()
            cross_attention()
            swiglu(False, False, False)
            for t in range(2):
                act.dma_start(mem_rows[:, t, :], mem[0, t * P:(t + 1) * P, :]).then_inc(mem_landed, 16)
            act.dma_start(mem_gain, xa_mem_norm[1, :].partition_broadcast(P)).then_inc(mem_landed, 16)
            swiglu(True, False, False)
            odd_mixer()
            cross_attention()
            swiglu(False, False, True)
            squares_of(1, h, True)

        @block.vector
        def _(dve):
            c = Tally()

            def split(k):
                for _ in range(k):
                    n = c.n["blk"]
                    if n >= TOTAL_BLOCKS:
                        return
                    c.add("blk")
                    dve.wait_ge(blk_hi, c.at("blk"))
                    nc.vector.tensor_tensor(w_lo[:, n % RING, :], w_raw[:, n % RAW, :],
                                            w_hi[:, n % RING, :].bitcast(F32), ALU.subtract).then_inc(blk_ready, 1)

            def chained(ins):
                ins.then_inc(step, 1)
                c.add("step")
                dve.wait_ge(step, c.n["step"])

            def next_mm():
                bank = mm_bank[c.n["mm"] % 2]
                c.add("mm")
                dve.wait_ge(mm_done, c.at("mm"))
                return bank

            def next_tr():
                bank = tr_bank[c.n["tr"] % 2]
                c.add("tr")
                c.add("tr_hi")
                dve.wait_ge(tr_hi, c.at("tr_hi"))
                return bank

            def skip_mm(k=1):
                c.add("mm", k)
                c.add("mm_read_act", k)

            def gated(t):
                bank = mm_bank[c.n["mm"] % 2]
                c.add("mm")
                c.add("silu")
                dve.wait_ge(silu_done, c.at("silu"))
                c.add("mm_read_dve")
                nc.vector.tensor_tensor(hid[:, t, :], hid[:, t, :], bank[:, FG:2 * FG],
                                        ALU.mult).then_inc(mm_read_dve, 1)

            def lo_hid(t):
                bank = next_tr()
                nc.vector.tensor_tensor(hidT_lo[:, t, :, :], bank[:, 0:FG].rearrange("p (a b) -> p a b", b=P),
                                        hidT_hi[:, t, :, :].bitcast(F32), ALU.subtract).then_inc(tr_read_dve, 1)
                c.add("tr_read_dve")

            def lo_rows(t, dst, hi, chunks=(0, 4)):
                for k in chunks:
                    bank = next_tr()
                    part = slice(t * P, (t + 1) * P)
                    nc.vector.tensor_tensor(dst[:, k:k + 4, part], bank[:, :].rearrange("p (a b) -> p a b", b=P),
                                            hi[:, k:k + 4, part].bitcast(F32),
                                            ALU.subtract).then_inc(tr_read_dve, 1)
                    c.add("tr_read_dve")

            def residual(t, scale):
                c.add("acc")
                dve.wait_ge(acc_done, c.n["acc"])
                for half in range(2):
                    cols = slice(half * HALF, (half + 1) * HALF)
                    nc.vector.scalar_tensor_tensor(out=h[:, t, cols], in0=acc[t][:, cols], scalar=scale,
                                                   in1=h[:, t, cols], op0=ALU.mult,
                                                   op1=ALU.add).then_inc(h_ready, 1)
                c.add("h", 2)

            def mean_square(t, eps=RMS_EPS):
                c.add("ssq", 2)
                dve.wait_ge(ssq_ready, c.n["ssq"])
                nc.vector.tensor_scalar(ms[:, t:t + 1], ssq[:, t, 0:1], ssq[:, t, 1:2], eps, ALU.add,
                                        ALU.add).then_inc(ms_ready, 1)

            def normed(t, src, g, wait_gain=False):
                c.add("norm")
                dve.wait_ge(rstd_ready, c.n["norm"])
                if wait_gain:
                    c.add("gain", 16)
                    dve.wait_ge(gain_landed, c.n["gain"])
                for half in range(2):
                    cols = slice(half * HALF, (half + 1) * HALF)
                    nc.vector.scalar_tensor_tensor(out=xn[:, t, cols], in0=src[:, t, cols], scalar=rstd[:, t:t + 1],
                                                   in1=g[:, cols], op0=ALU.mult, op1=ALU.mult).then_inc(xn_ready, 1)
                c.add("xn", 2)

            def swiglu(scale_before, with_mem, start, last):
                if not start:
                    residual(1, scale_before)
                mean_square(1)
                normed(1, h, gain)
                if start:
                    split(4)
                gated(0)
                if start:
                    split(2)
                lo_hid(0)
                gated(0)
                lo_rows(1, act_lo, act_hi)
                if start:
                    split(2)
                split(3)
                gated(1)
                split(1)
                if start:
                    bank = tr_bank[c.n["tr"] % 2]
                    c.add("tr")
                    dve.wait_ge(tr_done, c.n["tr"])
                    c.add("tr_read_dve")
                    nc.vector.tensor_copy(prmT[:, :, :], bank[:, :].rearrange("p (a b) -> p a b", b=P)[:, :, 0:40]
                                          ).then_inc(tr_read_dve, 1)
                lo_hid(0)

                def one_step(with_mem=False):
                    if with_mem:
                        mean_square(0)
                        normed(0, mem_rows, mem_gain)
                    gated(0)
                    if with_mem:
                        mean_square(1)
                    lo_hid(1)
                    if with_mem:
                        lo_rows(0, mem_lo, mem_hi)
                        normed(1, mem_rows, mem_gain)
                    split(3)
                    gated(1)
                    split(1)
                    lo_hid(0)
                    split(2)
                    if with_mem:
                        lo_rows(1, mem_lo, mem_hi)

                one_step(with_mem)
                turns = TURNS - 1 if last else TURNS
                with dve.Fori(0, turns) as turn:
                    c.turn = turn
                    for _ in range(TURN_STEPS):
                        one_step()
                    c.leave_loop(turns)
                if last:
                    for _ in range(TURN_STEPS):
                        one_step()
                residual(0, 0.5)
                lo_hid(1)
                split(1)
                mean_square(0)
                split(1)
                normed(0, h, gain, True)
                split(1)
                gated(1)
                split(1)
                lo_hid(1)
                split(2)
                if not last:
                    lo_rows(0, act_lo, act_hi)
                split(2)

            def out_rows(turn_inside=False):
                residual(0, 1.0)
                mean_square(0)
                normed(0, h, gain, True)
                split(4)
                if turn_inside:
                    lo_rows(0, act_lo, act_hi)
                split(4)

            def mixer_head():
                residual(1, 0.5)
                mean_square(1)
                normed(1, h, gain)
                skip_mm(3)
                split(3)
                lo_rows(1, act_lo, act_hi)
                skip_mm()
                split(1)

            def even_mixer():
                mixer_head()
                nc.vector.memset(aT[:, :, 0:TAPS - 1], 0.0).then_inc(pad_zero, 1)
                dve.wait_ge(pad_zero, 1)
                tokens = []

                def taps():
                    order = [1] * 6 + [2, 1] * 5
                    left = {1: TAPS, 2: TAPS, 3: POOL_TAP}
                    while any(order.count(n) < k for n, k in left.items()):
                        order += [n for n in (2, 3, 1) if order.count(n) < left[n]]
                    tap_of, last = {1: 0, 2: 0, 3: 0}, {}
                    for n in order:
                        k = tap_of[n]
                        tap_of[n] += 1
                        taken = aT[:, n, k:k + TOK]
                        if k == 0:
                            dve.wait_ge(mm_read_dve, tokens[n])
                            nc.vector.tensor_scalar(conv[:, n, :], taken, prmT[:, n, 0:1], prmT[:, n, 31:32],
                                                    ALU.mult, ALU.add).then_inc(conv_step, 1)
                        else:
                            dve.wait_ge(conv_step, last[n])
                            nc.vector.scalar_tensor_tensor(out=conv[:, n, :], in0=taken, scalar=prmT[:, n, k:k + 1],
                                                           in1=conv[:, n, :], op0=ALU.mult,
                                                           op1=ALU.add).then_inc(conv_step, 1)
                        c.add("conv")
                        last[n] = c.n["conv"]
                        yield

                conv_taps = taps()

                def tap(k):
                    for _ in range(k):
                        next(conv_taps, None)

                for n in range(CH // P):
                    skip_mm()
                    split(1)
                    bank = next_mm()
                    dve.wait_ge(mm_read_act, c.n["mm_read_act"])
                    c.add("mm_read_dve")
                    nc.vector.tensor_tensor(aT[:, n, TAPS - 1:TAPS - 1 + TOK], sig, bank[:, 0:TOK],
                                            ALU.mult).then_inc(mm_read_dve, 1)
                    tokens.append(c.n["mm_read_dve"])
                    split(1)
                    if n >= 1:
                        tap(6)
                for n in range(QH // KVH + 2):
                    skip_mm()
                    split(1)
                    tap(4 if n <= QH // KVH else 2)
                skip_mm()

                slopes = [2.0 ** (-8.0 * (hd + 1) / QH) for hd in range(QH)]

                def scores(t, first, count, width):
                    bank = next_mm()
                    c.add("mm_read_dve")
                    away = dist[:, 2 * P - width:2 * P]
                    for i in range(count):
                        hd = first + i
                        ins = nc.vector.scalar_tensor_tensor(
                            out=swa_p[t][:, hd * width:(hd + 1) * width], in0=away, scalar=-slopes[hd] * HD ** 0.5,
                            in1=bank[:, i * width:(i + 1) * width], op0=ALU.mult, op1=ALU.add)
                    ins.then_inc(mm_read_dve, 1)
                    dve.wait_ge(mm_read_dve, c.n["mm_read_dve"])
                    heads = slice(first, first + count)
                    p = swa_p[t].rearrange("p (a b) -> p a b", b=width)[:, heads, :]
                    chained(nc.vector.tensor_reduce(top[:, t, heads], p, AX.X, ALU.max))

                def maxima(t):
                    chained(nc.vector.scalar_tensor_tensor(out=neg[:, t, :], in0=top[:, t, :], scalar=HD ** -0.5,
                                                           in1=sink[:, :], op0=ALU.mult, op1=ALU.max))
                    chained(nc.vector.tensor_tensor(top[:, t, :], sink[:, :], neg[:, t, :], ALU.subtract))
                    nc.vector.tensor_scalar(neg[:, t, :], neg[:, t, :], -1.0, None, ALU.mult).then_inc(top_ready, 1)

                def sums(t):
                    c.add("exp", QH + 1)
                    dve.wait_ge(exp_done, c.n["exp"])
                    chained(nc.vector.tensor_tensor(den[:, t, :], den[:, t, :], esink[:, t, :], ALU.add))
                    chained(nc.vector.reciprocal(rinv[:, t, :], den[:, t, :]))

                def heads_out(t):
                    bank = next_mm()
                    c.add("mm_read_dve")
                    nc.vector.tensor_tensor(xn[:, t, 0:HALF].rearrange("p (a b) -> p a b", b=HD),
                                            bank[:, :].rearrange("p (a b) -> p a b", b=HD),
                                            rinv[:, t, :].unsqueeze(2).broadcast_to([P, QH, HD]),
                                            ALU.mult).then_inc(mm_read_dve, 1)

                skip_mm()
                for first in (0, 4):
                    scores(0, first, 4, P)
                maxima(0)
                split(1)
                tap(1)
                skip_mm()
                for first in (0, 2):
                    scores(1, first, 2, 2 * P)
                split(1)
                tap(6)
                sums(0)
                skip_mm()
                scores(1, 4, 2, 2 * P)
                heads_out(0)
                scores(1, 6, 2, 2 * P)
                maxima(1)
                split(1)
                tap(12)
                skip_mm()
                split(1)
                c.add("tr", 2)
                lo_rows(0, act_lo, act_hi, (4,))
                tap(14)
                skip_mm()
                c.add("tr", 4)
                sums(1)
                skip_mm()
                tap(15)
                heads_out(1)
                tap(CH // P * TAPS)
                dve.wait_ge(conv_step, c.n["conv"])
                dve.wait_ge(pool_conv, 2 * TAPS - POOL_TAP)
                c.add("conv")
                nc.vector.tensor_tensor(conv[:, 3, :], conv[:, 3, :], conv_part, ALU.add).then_inc(conv_step, 1)
                lo_rows(1, act_lo, act_hi, (4,))
                bank = next_mm()
                c.add("mm_read_dve")
                over_chunks = [P, CH // P, TOK]
                nc.vector.tensor_tensor(centred, conv, bank[:, 0:TOK].unsqueeze(1).broadcast_to(over_chunks),
                                        ALU.subtract).then_inc(mm_read_dve, 1)
                split(2)
                bank = next_mm()
                nc.vector.tensor_scalar(var, bank[:, 0:2], LN_EPS, None, ALU.add).then_inc(ln_dve, 1)
                dve.wait_ge(ln_pool, 1)
                for t in range(2):
                    nc.vector.tensor_scalar(diag[:, t, :], ident[:, :], rs[:, t:t + 1], float(CH), ALU.mult,
                                            ALU.mult).then_inc(ln_dve, 1)
                split(2)
                bank = next_mm()
                for n in range(CH // P):
                    nc.vector.tensor_tensor(centred[:, n, :], centred[:, n, :], bank[:, 0:TOK],
                                            ALU.mult).then_inc(scaled, 1)
                for n in range(CH // P):
                    dve.wait_ge(y_hi, n + 1)
                    nc.vector.tensor_tensor(act_lo[:, n, :], ln_out[:, n, :], act_hi[:, n, :].bitcast(F32),
                                            ALU.subtract).then_inc(y_ready, 1)
                split(4)
                residual(0, 1.0)
                mean_square(0)
                normed(0, h, gain, True)
                split(4)

            def odd_mixer():
                mixer_head()
                nc.vector.memset(pT[:, :, 0:SC_TAPS - 1], 0.0).then_inc(pad_zero, 1)
                dve.wait_ge(pad_zero, 2)
                for n in range(KD):
                    skip_mm()
                    split(1)
                    bank = next_mm()
                    c.add("mm_read_dve")
                    dve.wait_ge(mm_read_act, c.n["mm_read_act"])
                    nc.vector.tensor_tensor(pT[:, n, SC_TAPS - 1:SC_TAPS - 1 + TOK], gate_c, bank[:, 0:TOK],
                                            ALU.mult).then_inc(mm_read_dve, 1)
                    dve.wait_ge(mm_read_dve, c.n["mm_read_dve"])
                    w = prmT[:, n % 4, 34 + 3 * (n // 4):37 + 3 * (n // 4)]
                    chained(nc.vector.tensor_scalar(sc_acc, pT[:, n, 0:TOK], w[:, 0:1], None, ALU.mult))
                    split(1)
                    for k in range(1, SC_TAPS):
                        chained(nc.vector.scalar_tensor_tensor(out=sc_acc, in0=pT[:, n, k:k + TOK],
                                                               scalar=w[:, k:k + 1], in1=sc_acc, op0=ALU.mult,
                                                               op1=ALU.add))
                    bank = next_mm()
                    c.add("mm_read_dve")
                    nc.vector.tensor_tensor(sc_y[:, n, :], sc_acc, bank[:, 0:TOK], ALU.mult).then_inc(mm_read_dve, 1)
                    split(1)
                dve.wait_ge(mm_read_dve, c.n["mm_read_dve"])
                for n in range(4):
                    skip_mm()
                    split(1)
                for n in range(2):
                    dve.wait_ge(y_hi, CH // P + 1 + n)
                    nc.vector.tensor_tensor(act_lo[:, 4 * n:4 * n + 4, :], sc_y[:, 4 * n:4 * n + 4, :],
                                            act_hi[:, 4 * n:4 * n + 4, :].bitcast(F32),
                                            ALU.subtract).then_inc(y_ready, 1)
                skip_mm(2)
                split(4)
                out_rows()

            def cross_attention():
                residual(1, 1.0)
                mean_square(1)
                normed(1, h, gain)
                skip_mm()
                lo_rows(0, act_lo, act_hi)
                skip_mm()
                lo_rows(1, act_lo, act_hi)
                split(1)

                def maxima(hd):
                    bank = next_mm()
                    s = bank[:, :].rearrange("p (a b) -> p a b", b=MEM)
                    chained(nc.vector.tensor_reduce(top[:, :, hd], s, AX.X, ALU.max))
                    nc.vector.tensor_scalar(neg[:, :, hd], top[:, :, hd], -(XHD ** -0.5), None,
                                            ALU.mult).then_inc(top_ready, 1)

                def probs(hd):
                    c.add("exp", 2)
                    dve.wait_ge(exp_done, c.n["exp"])
                    chained(nc.vector.reciprocal(rinv[:, :, hd], den[:, :, hd]))
                    nc.vector.tensor_tensor(xa_p[:, hd, :, :], xa_p[:, hd, :, :],
                                            rinv[:, :, hd].unsqueeze(2).broadcast_to([P, 2, MEM]),
                                            ALU.mult).then_inc(probs_ready, 1)

                def lo_out(hd):
                    bank = next_mm()
                    c.add("mm_read_dve")
                    c.add("out_hi")
                    dve.wait_ge(out_hi, c.n["out_hi"])
                    part = slice(2 * hd, 2 * hd + 2)
                    nc.vector.tensor_tensor(mem_lo[:, part, :], bank[:, :].rearrange("p (a b) -> p a b", b=TOK),
                                            mem_hi[:, part, :].bitcast(F32), ALU.subtract).then_inc(mm_read_dve, 1)

                def queries(n):
                    skip_mm()
                    split(QUERY_SPLITS[n])

                queries(0)
                for hd in range(XH):
                    queries(2 * hd + 1)
                    if hd + 1 < XH:
                        queries(2 * hd + 2)
                    if hd >= 2:
                        lo_out(hd - 2)
                    maxima(hd)
                    probs(hd)
                    c.add("tr")
                lo_out(XH - 2)
                lo_out(XH - 1)
                out_rows(True)

            nc.vector.memset(prm, 0.0).then_inc(prm_zero, 1)
            dve.wait_ge(const_ready, 3)
            nc.vector.tensor_copy(dist[:, :], dist_int.bitcast(I32)).then_inc(dist_ready, 1)
            mean_square(0)
            normed(0, h, gain, True)
            split(1)
            lo_rows(0, act_lo, act_hi)
            split(3)
            swiglu(None, True, True, False)
            even_mixer()
            cross_attention()
            swiglu(1.0, False, False, False)
            swiglu(0.5, True, False, False)
            odd_mixer()
            cross_attention()
            swiglu(1.0, False, False, True)
            residual(1, 0.5)
            mean_square(1)
            normed(1, h, gain)

        @block.tensor
        def _(pe):
            c = Tally()
            mm_free = [None, None]
            tr_free = [None, None]

            def start_mm():
                if c.turn is not None:
                    pe.wait_ge(mm_read_dve, c.at("mm_read_dve", 1))
                elif mm_free[0]:
                    pe.wait_ge(*mm_free[0])
                return mm_bank[c.n["mm"] % 2]

            def end_mm(ins, reader):
                ins.then_inc(mm_done, 1)
                c.add("mm")
                if isinstance(reader, tuple):
                    freed = reader
                elif reader == "dve":
                    c.add("mm_read_dve")
                    freed = (mm_read_dve, c.n["mm_read_dve"])
                else:
                    c.add("mm_read_act")
                    freed = (mm_read_act, c.n["mm_read_act"])
                mm_free[0], mm_free[1] = mm_free[1], freed

            def start_tr():
                if c.turn is not None:
                    pe.wait_ge(tr_read_dve, c.at("tr_read_dve", 1))
                elif tr_free[0]:
                    pe.wait_ge(*tr_free[0])
                return tr_bank[c.n["tr"] % 2]

            def end_tr(ins, reader="dve"):
                ins.then_inc(tr_done, 1)
                c.add("tr")
                name, s = ("tr_read_dve", tr_read_dve) if reader == "dve" else ("tr_read_act", tr_read_act)
                c.add(name)
                tr_free[0], tr_free[1] = tr_free[1], (s, c.n[name])

            def take(n):
                value = n + 1
                if c.turn is not None:
                    value = value + c.turn * PER_TURN["blk"]
                pe.wait_ge(blk_ready, value)

            def products(out_ap, stat, mov, first, last):
                pairs = ((stat[0], mov[0]), (stat[0], mov[1]), (stat[1], mov[0]))
                for i, (a, b) in enumerate(pairs):
                    ins = nc.tensor.matmul(out_ap, a, b, start=first and i == 0, stop=last and i == 2)
                return ins

            def tile_of(pair, k, t):
                return tuple(a[:, k, t * P:(t + 1) * P] for a in pair)

            act_pair, mem_pair = (act_hi, act_lo), (mem_hi, mem_lo)

            def gate_up(t, n, final):
                bank = start_mm()
                for kk in range(4):
                    if not final:
                        take(n + kk)
                    for j in range(2):
                        k = 2 * kk + j
                        cols = slice(j * HALF, (j + 1) * HALF)
                        slot = (n + kk) % RING
                        ins = products(bank[:, :], tile_of(act_pair, k, t), (w_hi[:, slot, cols], w_lo[:, slot, cols]),
                                       k == 0, k == KD - 1)
                    if kk < 3 and final:
                        ins.then_inc(blk_used, 1)
                end_mm(ins, "dve")

            def gu(t, n):
                gate_up(t, n, t == 1)

            def turn_hid(t, job):
                bank = start_tr()
                pe.wait_ge(mm_read_dve, c.at("mm_read_dve", job))
                for i in range(FG // P):
                    ins = nc.tensor.transpose(bank[:, i * P:(i + 1) * P], hid[:, t, i * P:(i + 1) * P], ident[:, :])
                end_tr(ins)

            def down(t, n, back, first=False, last=False):
                pe.wait_ge(tr_read_dve, c.at("tr_read_dve", back))
                for i in range(2):
                    if t == 0:
                        take(n + i)
                    down_chunk(t, n + i, (hidT_hi[:, t, i, :], hidT_lo[:, t, i, :]), first and i == 0,
                               last and i == 1)

            def down_chunk(t, n, stat, first, last):
                slot = n % RING
                for half in range(2):
                    cols = slice(half * HALF, (half + 1) * HALF)
                    ins = products(acc[t][:, cols], stat, (w_hi[:, slot, cols], w_lo[:, slot, cols]), first, last)
                if last:
                    ins.then_inc(acc_done, 1)
                elif t == 1:
                    ins.then_inc(blk_used, 1)

            def acc_free(t):
                if c.n["sums"]:
                    pe.wait_ge(h_ready, 4 * (c.n["sums"] - 1) + 2 * (t + 1))

            def turn_rows(t):
                for k in (0, 4):
                    bank = start_tr()
                    c.add("xn")
                    pe.wait_ge(xn_ready, c.n["xn"])
                    for j in range(4):
                        src = (k + j) * P
                        ins = nc.tensor.transpose(bank[:, j * P:(j + 1) * P], xn[:, t, src:src + P], ident[:, :])
                    end_tr(ins)

            def swiglu(with_mem, start, last):
                n = c.n["blk"]
                sums = c.n["sums"]
                pe.wait_ge(tr_read_dve, c.n["tr_read_dve"])
                gu(0, n)
                gu(0, n + 4)
                turn_hid(0, 1)
                turn_rows(1)
                acc_free(0)
                down(0, n + 8, 2, first=True)
                pe.wait_ge(tr_read_dve, c.n["tr_read_dve"])
                gu(1, n)
                if start:
                    bank = start_tr()
                    pe.wait_ge(prm_landed, 16 * 7)
                    for j in range(4):
                        ins = nc.tensor.transpose(bank[:, j * P:(j + 1) * P], prm[:, j * P:(j + 1) * P], ident[:, :])
                    end_tr(ins)

                turn_hid(0, 1)

                def one_step(m, first=False, with_mem=False):
                    gu(0, m)
                    down(0, m + 4, 0)
                    turn_hid(1, 1)
                    if with_mem:
                        turn_rows(0)
                    gu(1, m - 6)
                    turn_hid(0, 1)
                    if first:
                        acc_free(1)
                    down(1, m - 2, 3 if with_mem else 1, first=first)
                    if with_mem:
                        turn_rows(1)

                one_step(n + 10, True, with_mem)
                with pe.Fori(0, TURNS) as turn:
                    c.turn = turn
                    for u in range(TURN_STEPS):
                        one_step(n + 16 + 6 * u)
                    c.leave_loop()
                m = n + 4 + 6 * (GROUPS - 1)
                down(0, m, 0, last=True)
                turn_hid(1, 0)
                gu(1, m - 6)
                down(1, m - 2, 0)
                turn_hid(1, 0)
                if not last:
                    turn_rows(0)
                down(1, m, 0 if last else 2, last=True)
                c.n["blk"] = m + 2
                c.add("sums")

            def chunk(pair, reader):
                n = c.n["blk"]
                bank = start_mm()
                take(n)
                slot = n % RING
                for k in range(KD):
                    cols = slice(k * P, (k + 1) * P)
                    ins = products(bank[:, 0:TOK], (w_hi[:, slot, cols], w_lo[:, slot, cols]),
                                   (pair[0][:, k, :], pair[1][:, k, :]), k == 0, k == KD - 1)
                end_mm(ins, reader)
                c.add("blk")

            def values(before_end=None):
                n = c.n["blk"]
                for m in range(2):
                    bank = start_mm()
                    for kk in range(4):
                        take(n + kk)
                        if m == 1 and kk == 3 and before_end:
                            before_end()
                        for j in range(2):
                            k = 2 * kk + j
                            cols = slice(j * HALF, (j + 1) * HALF)
                            slot = (n + kk) % RING
                            ins = products(bank[:, :], tile_of(mem_pair, k, m),
                                           (w_hi[:, slot, cols], w_lo[:, slot, cols]), k == 0, k == KD - 1)
                    end_mm(ins, "act")
                    if m == 1:
                        c.add("blk", 4)
                    yield

            def out_rows(pair=act_pair, before=(), turn_inside=False):
                n = c.n["blk"]
                before = dict(before)
                for t in range(2):
                    acc_free(t)
                    for k in range(KD):
                        if t == 0:
                            take(n + k)
                            if k in before:
                                before[k]()
                        if t == 1 and k == 4 and turn_inside:
                            turn_rows(0)
                        down_chunk(t, n + k, tile_of(pair, k, t), k == 0, k == KD - 1)
                c.add("blk", KD)
                c.add("sums")

            def mixer_head():
                for _ in range(3):
                    chunk(mem_pair, "act")
                turn_rows(1)
                chunk(mem_pair, "act")
                pe.wait_ge(tr_read_dve, c.n["tr_read_dve"])

            def even_mixer():
                mixer_head()
                for _ in range(CH // P):
                    chunk(act_pair, "act")
                    chunk(act_pair, "dve")
                for _ in range(QH // KVH + 1):
                    chunk(act_pair, "act")
                n = c.n["blk"]
                take(n)
                for t in range(2):
                    bank = start_mm()
                    for k in range(KD):
                        cols = slice(k * P, (k + 1) * P)
                        ins = products(bank[:, 0:P], tile_of(act_pair, k, t),
                                       (w_hi[:, n % RING, cols], w_lo[:, n % RING, cols]), k == 0, k == KD - 1)
                    end_mm(ins, "act")
                c.add("blk")
                in_done = c.n["mm_read_act"]

                def scores(t, first, count):
                    bank = start_mm()
                    pe.wait_ge(mm_read_act, in_done)
                    keys = slice(0, (t + 1) * P)
                    width = (t + 1) * P
                    for i in range(count):
                        hd = first + i
                        kv = hd // (QH // KVH)
                        rows = slice(HD * kv, HD * (kv + 1))
                        ins = nc.tensor.matmul(bank[:, i * width:(i + 1) * width],
                                               swa_qT[rows, hd % (QH // KVH), t * P:(t + 1) * P],
                                               swa_kT[rows, keys], start=True, stop=True)
                    end_mm(ins, "dve")

                def turn_probs(t, n0, n1):
                    for n in range(n0, n1):
                        bank = start_tr()
                        pe.wait_ge(exp_done, (2 * n + 2 + QH + 1) if t else (4 * n + 4))
                        for j in range(4):
                            at = n * HALF + j * P
                            ins = nc.tensor.transpose(bank[:, j * P:(j + 1) * P], swa_p[t][:, at:at + P], ident[:, :])
                        end_tr(ins, "act")

                def heads_out(t):
                    bank = start_mm()
                    pe.wait_ge(tr_read_act, c.n["tr_read_act"])
                    for hd in range(QH):
                        kv = hd // (QH // KVH)
                        for j in range(t + 1):
                            at = (hd * (t + 1) + j) * P
                            ins = nc.tensor.matmul(bank[:, hd * HD:(hd + 1) * HD],
                                                   swa_pT[at // HALF][:, at % HALF:at % HALF + P],
                                                   swa_v[:, j, kv * HD:(kv + 1) * HD], start=j == 0, stop=j == t)
                    end_mm(ins, "dve")
                    return c.n["mm_read_dve"]

                def turn_out(t, ready):
                    bank = start_tr()
                    pe.wait_ge(mm_read_dve, ready)
                    for j in range(4):
                        ins = nc.tensor.transpose(bank[:, j * P:(j + 1) * P], xn[:, t, j * P:(j + 1) * P],
                                                  ident[:, :])
                    end_tr(ins)

                chunk(mem_pair, "act")
                for first in (0, 4):
                    scores(0, first, 4)
                chunk(mem_pair, "act")
                for first in (0, 2):
                    scores(1, first, 2)
                chunk(mem_pair, "act")
                turn_probs(0, 0, 2)
                scores(1, 4, 2)
                out0 = heads_out(0)
                scores(1, 6, 2)
                chunk(mem_pair, "act")
                turn_out(0, out0)
                operand0 = c.n["tr_read_dve"]
                fill = values()
                next(fill)
                turn_probs(1, 0, 2)
                next(fill)
                next(fill, None)
                turn_probs(1, 2, 4)
                n = c.n["blk"]

                def out_part(t, k):
                    at = n + (k + 4) % KD
                    if t == 0:
                        take(at)
                        if k < 4:
                            pe.wait_ge(y_ready, k + 1)
                    down_chunk(t, at, tile_of(act_pair, k, t), k == 4, k == 3)

                acc_free(0)
                pe.wait_ge(tr_read_dve, operand0)
                out_part(0, 4)
                out1 = heads_out(1)
                out_part(0, 5)
                turn_out(1, out1)
                bank = start_mm()
                pe.wait_ge(conv_step, 2 * TAPS + POOL_TAP + 1)
                pe.wait_ge(pool_conv, TAPS)
                for k in range(CH // P):
                    ins = nc.tensor.matmul(bank[:, 0:TOK], ones[:, :], conv[:, k, :], start=k == 0,
                                           stop=k == CH // P - 1)
                end_mm(ins, "dve")
                out_part(0, 6)
                out_part(0, 7)
                bank = start_mm()
                pe.wait_ge(ln_act, 1)
                for t in range(2):
                    for k in range(CH // P):
                        ins = nc.tensor.matmul(bank[:, t:t + 1], squares[:, k, t * P:(t + 1) * P], ones[:, 0:1],
                                               start=k == 0, stop=k == CH // P - 1)
                end_mm(ins, (ln_dve, 1))
                acc_free(1)
                pe.wait_ge(tr_read_dve, c.n["tr_read_dve"])
                out_part(1, 4)
                out_part(1, 5)
                bank = start_mm()
                pe.wait_ge(ln_dve, 3)
                ins = nc.tensor.matmul(bank[:, 0:TOK], ones[:, :], diag.rearrange("p a b -> p (a b)"), start=True,
                                       stop=True)
                end_mm(ins, (scaled, CH // P))
                out_part(1, 6)
                out_part(1, 7)
                for t in range(2):
                    for k in range(4):
                        out_part(t, k)
                c.add("blk", KD)
                c.add("sums")

            def odd_mixer():
                mixer_head()
                for _ in range(KD):
                    chunk(act_pair, "act")
                    chunk(act_pair, "dve")
                    chunk(act_pair, "dve")
                for _ in range(4):
                    chunk(mem_pair, "act")
                for _ in values():
                    pass
                out_rows(before={k: lambda half=half: pe.wait_ge(y_ready, CH // P + 1 + half)
                                 for half, k in enumerate((0, 4))})

            def cross_attention(n):
                fill = values(lambda: turn_rows(1))
                next(fill)
                turn_rows(0)
                next(fill)
                next(fill, None)
                exp_base = 2 * (QH + 1) + 2 * XH * n
                probs_read, out_read = {}, {}

                def scores(hd):
                    bank = start_mm()
                    pe.wait_ge(mm_read_act, c.n["mm_read_act"] - (1 if hd + 1 < XH else 0))
                    for t in range(2):
                        for q in (2 * hd, 2 * hd + 1):
                            ins = nc.tensor.matmul(bank[:, t * MEM:(t + 1) * MEM], xa_qT[:, q, t * P:(t + 1) * P],
                                                   keyT[:, q, :], start=q == 2 * hd, stop=q == 2 * hd + 1)
                    end_mm(ins, (exp_done, exp_base + 2 * (hd + 1)))

                def turn_probs(hd):
                    bank = start_tr()
                    pe.wait_ge(probs_ready, XH * n + hd + 1)
                    for m in range(2):
                        for t in range(2):
                            at = (2 * m + t) * P
                            ins = nc.tensor.transpose(bank[:, at:at + P], xa_p[:, hd, t, m * P:(m + 1) * P],
                                                      ident[:, :])
                    end_tr(ins, "act")
                    probs_read[hd] = c.n["tr_read_act"]

                def head_out(hd):
                    bank = start_mm()
                    pe.wait_ge(tr_read_act, probs_read[hd])
                    for f in range(2):
                        at = hd * XHD + f * P
                        for m in range(2):
                            ins = nc.tensor.matmul(bank[:, f * TOK:(f + 1) * TOK], val[:, m, at:at + P],
                                                   xa_pT[:, hd, m, :], start=m == 0, stop=m == 1)
                    end_mm(ins, "dve")
                    out_read[hd] = c.n["mm_read_dve"]

                pe.wait_ge(tr_read_dve, c.n["tr_read_dve"])
                chunk(act_pair, "act")
                for hd in range(XH):
                    chunk(act_pair, "act")
                    if hd + 1 < XH:
                        chunk(act_pair, "act")
                    if hd >= 2:
                        head_out(hd - 2)
                    if hd >= 1:
                        turn_probs(hd - 1)
                    scores(hd)
                head_out(XH - 2)

                def operand(hd):
                    return lambda: pe.wait_ge(mm_read_dve, out_read[hd])

                out_rows(mem_pair, {0: operand(0), 2: operand(1), 3: lambda: turn_probs(XH - 1), 4: operand(XH - 2),
                                    5: lambda: head_out(XH - 1), 6: operand(XH - 1)}, True)

            pe.wait_ge(const_ready, 1)
            turn_rows(0)
            swiglu(True, True, False)
            even_mixer()
            cross_attention(0)
            swiglu(False, False, False)
            swiglu(True, False, False)
            odd_mixer()
            cross_attention(1)
            swiglu(False, False, True)


_INS = ["x", "mem", "ffn1_norm", "ffn1_w_gu", "ffn1_w_down", "mix_norm", "even_w_in", "conv_a_w", "conv_a_b",
        "conv_a_ln_g", "conv_a_ln_b", "swa_sinks", "even_w_out", "odd_w_in", "sc_conv_w", "odd_w_out", "xa_norm",
        "xa_mem_norm", "xa_wq", "xa_wkv", "xa_wo", "ffn2_norm", "ffn2_w_gu", "ffn2_w_down", "final_norm"]


def kernel(**inputs):
    import numpy as np
    import concourse.bacc as bacc
    from concourse.bass_utils import run_bass_kernel_spmd

    nc = bacc.Bacc("TRN2", target_bir_lowering=False, num_devices=1, dynamic_dma_scratch_size=256)
    arrays, args = {}, []
    for name in _INS:
        a = np.ascontiguousarray(inputs[name])
        arrays[f"in_{name}"] = a
        args.append(nc.dram_tensor(f"in_{name}", a.shape, mybir.dt.from_np(a.dtype), kind="ExternalInput").ap())
    out = nc.dram_tensor("out_0", (1, TOK, D), F32, kind="ExternalOutput").ap()
    trunk(nc, *args, out)
    r = run_bass_kernel_spmd(nc, [arrays], core_ids=[0])
    return r.results[0]["out_0"]
```
